# Optimizing a Trainium2 kernel written in Bass

```python
import jax, jax.numpy as jnp
from jax import lax
import numpy as np

D_MODEL = 1024
BATCH = 1
SEQ = 512
DEPTH = 2

N_MIXERS = 2
N_LAYERS_A = (DEPTH + 1) // 2
N_LAYERS_B = DEPTH // 2
PLE_DIM = 256
CONV_A_WIDTH = 3
D_RNN = D_MODEL
LRU_BLOCK = 256
N_LRU_BLOCKS = D_RNN // LRU_BLOCK
CONV_B_WIDTH = 4
RG_C = 8.0
N_GROUPS = 4
EXPERTS_PER_GROUP = 8
N_EXPERTS = N_GROUPS * EXPERTS_PER_GROUP
TOP_K = 2
D_EXPERT = 512
ROUTE_BLOCK = 128
EPS = 1e-6


def rmsnorm(x, g):
    x32 = x.astype(jnp.float32)
    y = x32 * lax.rsqrt(jnp.mean(x32 * x32, axis=-1, keepdims=True) + EPS)
    return (y * g.astype(jnp.float32)).astype(x.dtype)

def depthwise_conv(x, w, pad):
    return lax.conv_general_dilated(
        x, w[:, None, :], window_strides=(1,), padding=[pad],
        dimension_numbers=('NWC', 'WIO', 'NWC'), feature_group_count=x.shape[-1])

def short_conv_mixer(xn, w_in, conv_w, w_out):
    bgate, cgate, h = jnp.split(xn @ w_in, 3, axis=-1)
    u = depthwise_conv(cgate * h, conv_w, (1, 1))
    return (bgate * u) @ w_out

def _linear_combine(earlier, later):
    a_e, b_e = earlier
    a_l, b_l = later
    return a_l * a_e, a_l * b_e + b_l

def rglru_direction(uh, w_r, b_r, w_i, b_i, lam, reverse):
    bsz, s, nh, dh = uh.shape
    u = uh.reshape(bsz, s, nh * dh)
    r = jax.nn.sigmoid((jnp.einsum('bshd,hde->bshe', uh, w_r).reshape(bsz, s, -1) + b_r).astype(jnp.float32))
    i = jax.nn.sigmoid((jnp.einsum('bshd,hde->bshe', uh, w_i).reshape(bsz, s, -1) + b_i).astype(jnp.float32))
    log_a = -RG_C * r * jax.nn.softplus(-lam.astype(jnp.float32))
    a = jnp.exp(log_a)
    gated = jnp.sqrt(-jnp.expm1(2.0 * log_a)) * (i * u.astype(jnp.float32))
    _, h = lax.associative_scan(_linear_combine, (a, gated), axis=1, reverse=reverse)
    return h.astype(uh.dtype)

def rglru_mixer(xn, w_in, conv_w, conv_bias, w_rg, b_rg, w_ig, b_ig, lam, w_out):
    y_branch, u = jnp.split(xn @ w_in, 2, axis=-1)
    y_branch = jax.nn.gelu(y_branch)
    u = depthwise_conv(u, conv_w, (2, 1)) + conv_bias
    bsz, s, _ = u.shape
    uh = u.reshape(bsz, s, N_LRU_BLOCKS, LRU_BLOCK)
    h = (rglru_direction(uh, w_rg[0], b_rg[0], w_ig[0], b_ig[0], lam[0], False)
         + rglru_direction(uh, w_rg[1], b_rg[1], w_ig[1], b_ig[1], lam[1], True))
    return (y_branch * h) @ w_out

def hier_moe(x, w_rg, b_rg, w_re, b_re, w_gate, w_up, w_down):
    bsz, s, d = x.shape
    n = bsz * s
    xf = x.reshape(n, d)
    pg = jax.nn.softmax((xf @ w_rg).astype(jnp.float32) + b_rg.astype(jnp.float32), axis=-1)
    pg_top, g_top = lax.top_k(pg, 1)
    le = ((xf @ w_re).astype(jnp.float32) + b_re.astype(jnp.float32)).reshape(n, N_GROUPS, EXPERTS_PER_GROUP)
    le_sel = jnp.take_along_axis(le, g_top[:, :, None], axis=1)[:, 0]
    pe = jax.nn.softmax(le_sel, axis=-1)
    top_p, top_i = lax.top_k(pe, TOP_K)
    top_p = top_p / jnp.sum(top_p, axis=-1, keepdims=True)
    expert = g_top * EXPERTS_PER_GROUP + top_i
    weight = pg_top * top_p

    n_slots = n * TOP_K
    e_flat = expert.reshape(-1)
    tok_flat = jnp.arange(n_slots, dtype=jnp.int32) // TOP_K
    w_flat = weight.reshape(-1)
    order = jnp.argsort(e_flat)
    e_sorted = e_flat[order]
    counts = jnp.bincount(e_flat, length=N_EXPERTS)
    start = jnp.cumsum(counts) - counts
    padded = ((counts + ROUTE_BLOCK - 1) // ROUTE_BLOCK) * ROUTE_BLOCK
    pend = jnp.cumsum(padded)
    pstart = pend - padded
    dest = pstart[e_sorted] + (jnp.arange(n_slots) - start[e_sorted])
    n_blocks = -(-n_slots // ROUTE_BLOCK) + N_EXPERTS
    slot_of_pos = jnp.full((n_blocks * ROUTE_BLOCK,), n_slots, jnp.int32).at[dest].set(order.astype(jnp.int32))
    tok_pad = jnp.concatenate([tok_flat, jnp.array([n], jnp.int32)])[slot_of_pos]
    w_pad = jnp.concatenate([w_flat, jnp.zeros((1,), jnp.float32)])[slot_of_pos]
    block_expert = jnp.clip(jnp.searchsorted(pend, jnp.arange(n_blocks) * ROUTE_BLOCK, side='right'), 0, N_EXPERTS - 1)
    x_pad = jnp.concatenate([xf, jnp.zeros((1, d), xf.dtype)], axis=0)

    def expert_block(args):
        idx, e = args
        xb = x_pad[idx]
        hb = jax.nn.silu(xb @ w_gate[e]) * (xb @ w_up[e])
        return hb @ w_down[e]

    y_blocks = lax.map(expert_block, (tok_pad.reshape(n_blocks, ROUTE_BLOCK), block_expert))
    contrib = y_blocks.reshape(-1, d) * w_pad[:, None].astype(x.dtype)
    y = jnp.zeros((n + 1, d), x.dtype).at[tok_pad].add(contrib)
    return y[:n].reshape(bsz, s, d)

def _normal(key, shape, fan_in):
    return jax.random.normal(key, shape, jnp.float32) * (fan_in ** -0.5)

def first_inputs(seed: int = 0) -> dict:
    key = jax.random.key(seed)
    ks = jax.random.split(key, 28)
    f32 = jnp.float32
    D, R, H, Bk = D_MODEL, D_RNN, N_LRU_BLOCKS, LRU_BLOCK
    x = jax.random.normal(ks[0], (BATCH, SEQ, D), f32)
    p = jax.random.normal(ks[1], (DEPTH, BATCH, SEQ, PLE_DIM), f32)
    norm_mix = 1.0 + 0.05 * jax.random.normal(ks[2], (DEPTH, D), f32)
    w_in_a = _normal(ks[3], (N_LAYERS_A, D, 3 * D), D)
    conv_a = _normal(ks[4], (N_LAYERS_A, CONV_A_WIDTH, D), CONV_A_WIDTH)
    w_out_a = _normal(ks[5], (N_LAYERS_A, D, D), D)
    w_in_b = _normal(ks[6], (N_LAYERS_B, D, 2 * R), D)
    conv_b = _normal(ks[7], (N_LAYERS_B, CONV_B_WIDTH, R), CONV_B_WIDTH)
    conv_bias_b = 0.01 * jax.random.normal(ks[8], (N_LAYERS_B, R), f32)
    w_rgate_b = _normal(ks[9], (N_LAYERS_B, 2, H, Bk, Bk), Bk)
    b_rgate_b = 0.01 * jax.random.normal(ks[10], (N_LAYERS_B, 2, R), f32)
    w_igate_b = _normal(ks[11], (N_LAYERS_B, 2, H, Bk, Bk), Bk)
    b_igate_b = 0.01 * jax.random.normal(ks[12], (N_LAYERS_B, 2, R), f32)
    a0 = jax.random.uniform(ks[13], (N_LAYERS_B, 2, R), f32, minval=0.9, maxval=0.999)
    sig = a0 ** (1.0 / RG_C)
    lam_b = jnp.log(sig) - jnp.log1p(-sig)
    w_out_b = _normal(ks[14], (N_LAYERS_B, R, D), R)
    norm_ffn = 1.0 + 0.05 * jax.random.normal(ks[15], (DEPTH, D), f32)
    w_router_group = _normal(ks[16], (DEPTH, D, N_GROUPS), D)
    b_router_group = 0.01 * jax.random.normal(ks[17], (DEPTH, N_GROUPS), f32)
    w_router_expert = _normal(ks[18], (DEPTH, D, N_EXPERTS), D)
    b_router_expert = 0.01 * jax.random.normal(ks[19], (DEPTH, N_EXPERTS), f32)
    w_exp_gate = _normal(ks[20], (DEPTH, N_EXPERTS, D, D_EXPERT), D)
    w_exp_up = _normal(ks[21], (DEPTH, N_EXPERTS, D, D_EXPERT), D)
    w_exp_down = _normal(ks[22], (DEPTH, N_EXPERTS, D_EXPERT, D), D_EXPERT)
    norm_ple = 1.0 + 0.05 * jax.random.normal(ks[23], (DEPTH, D), f32)
    w_ple = _normal(ks[24], (DEPTH, PLE_DIM, D), PLE_DIM)
    w_ple_gate = _normal(ks[25], (DEPTH, D, D), D)
    b_ple_gate = 0.01 * jax.random.normal(ks[26], (DEPTH, D), f32)
    norm_final = 1.0 + 0.05 * jax.random.normal(ks[27], (D,), f32)
    return {'x': x, 'p': p, 'norm_mix': norm_mix,
            'w_in_a': w_in_a, 'conv_a': conv_a, 'w_out_a': w_out_a,
            'w_in_b': w_in_b, 'conv_b': conv_b, 'conv_bias_b': conv_bias_b,
            'w_rgate_b': w_rgate_b, 'b_rgate_b': b_rgate_b,
            'w_igate_b': w_igate_b, 'b_igate_b': b_igate_b,
            'lam_b': lam_b, 'w_out_b': w_out_b, 'norm_ffn': norm_ffn,
            'w_router_group': w_router_group, 'b_router_group': b_router_group,
            'w_router_expert': w_router_expert, 'b_router_expert': b_router_expert,
            'w_exp_gate': w_exp_gate, 'w_exp_up': w_exp_up, 'w_exp_down': w_exp_down,
            'norm_ple': norm_ple, 'w_ple': w_ple, 'w_ple_gate': w_ple_gate,
            'b_ple_gate': b_ple_gate, 'norm_final': norm_final}

def first_block(x, p, norm_mix, w_in_a, conv_a, w_out_a, w_in_b, conv_b, conv_bias_b,
              w_rgate_b, b_rgate_b, w_igate_b, b_igate_b, lam_b, w_out_b, norm_ffn,
              w_router_group, b_router_group, w_router_expert, b_router_expert,
              w_exp_gate, w_exp_up, w_exp_down, norm_ple, w_ple, w_ple_gate,
              b_ple_gate, norm_final):
    h = x
    for i in range(DEPTH):
        xn = rmsnorm(h, norm_mix[i])
        j = i // N_MIXERS
        if i % N_MIXERS == 0:
            mix = short_conv_mixer(xn, w_in_a[j], conv_a[j], w_out_a[j])
        else:
            mix = rglru_mixer(xn, w_in_b[j], conv_b[j], conv_bias_b[j], w_rgate_b[j], b_rgate_b[j],
                              w_igate_b[j], b_igate_b[j], lam_b[j], w_out_b[j])
        h = h + mix
        h = h + hier_moe(rmsnorm(h, norm_ffn[i]), w_router_group[i], b_router_group[i],
                         w_router_expert[i], b_router_expert[i],
                         w_exp_gate[i], w_exp_up[i], w_exp_down[i])
        gate = jax.nn.sigmoid(rmsnorm(h, norm_ple[i]) @ w_ple_gate[i] + b_ple_gate[i])
        h = h + gate * (p[i] @ w_ple[i])
    return rmsnorm(h, norm_final)


DEPTH_2 = 1

HEAD_DIM = 64
MIX_WIDTH = D_MODEL
NSA_WIDTH = MIX_WIDTH // 2
DSA_WIDTH = MIX_WIDTH - NSA_WIDTH
NSA_HEADS = NSA_WIDTH // HEAD_DIM
NSA_KV_HEADS = 2
NSA_KV_W = NSA_KV_HEADS * HEAD_DIM
DSA_HEADS = DSA_WIDTH // HEAD_DIM
DSA_KV_HEADS = 2
DSA_KV_W = DSA_KV_HEADS * HEAD_DIM
IDX_HEADS = 4
IDX_DIM = 64
CMP_BLOCK = 32
CMP_STRIDE = 16
CMP_HIDDEN = 256
SEL_BLOCK = 64
SEL_TOPN = 16
WINDOW = 512
DSA_TOPK_MAX = 256
ROPE_THETA = 10000.0
Q_BLOCK = 128
SEL_Q_BLOCK = 64
NEG = -1e30
FORCE = 1e6
ATTN_SCALE = HEAD_DIM ** -0.5

IN_WIDTHS = (NSA_WIDTH, NSA_KV_W, NSA_KV_W, NSA_KV_W, NSA_KV_W, NSA_KV_W, NSA_KV_W,
             3 * NSA_HEADS, NSA_WIDTH,
             DSA_WIDTH, DSA_KV_W, DSA_KV_W, IDX_HEADS * IDX_DIM, IDX_DIM, IDX_HEADS, DSA_WIDTH)
IN_COLS = sum(IN_WIDTHS)


def rms_norm(x, gain):
    xf = x.astype(jnp.float32)
    y = xf * lax.rsqrt(jnp.mean(xf * xf, axis=-1, keepdims=True) + EPS)
    return (y * gain.astype(jnp.float32)).astype(x.dtype)

def rope(x, pos):
    half = x.shape[-1] // 2
    inv_freq = ROPE_THETA ** (-jnp.arange(half, dtype=jnp.float32) / half)
    ang = pos[:, None] * inv_freq[None, :]
    cos = jnp.cos(ang)[:, None, :]
    sin = jnp.sin(ang)[:, None, :]
    xf = x.astype(jnp.float32)
    x1, x2 = xf[..., :half], xf[..., half:]
    return jnp.concatenate([x1 * cos - x2 * sin, x2 * cos + x1 * sin], axis=-1).astype(x.dtype)

def masked_softmax(s, mask):
    s = jnp.where(mask, s.astype(jnp.float32), NEG)
    p = jax.nn.softmax(s, axis=-1)
    return jnp.where(mask, p, 0.0)

def split_columns(proj, widths):
    offsets = np.cumsum(np.array(widths))[:-1]
    return jnp.split(proj, [int(o) for o in offsets], axis=-1)

def compress(k_raw, pe, w1, b1, w2):
    B, S, G, Dh = k_raw.shape
    n_cmp = (S - CMP_BLOCK) // CMP_STRIDE + 1
    idx = jnp.arange(n_cmp)[:, None] * CMP_STRIDE + jnp.arange(CMP_BLOCK)[None, :]
    blocks = k_raw[:, idx] + pe[None, None, :, None, :]
    flat = blocks.transpose(0, 1, 3, 2, 4).reshape(B, n_cmp, G, CMP_BLOCK * Dh)
    hid = jax.nn.silu(flat @ w1 + b1)
    return hid @ w2

def compressed_branch(q, kc, vc):
    S = q.shape[1]
    n_cmp = kc.shape[1]
    cmp_end = jnp.arange(n_cmp) * CMP_STRIDE + CMP_BLOCK - 1
    t = jnp.arange(S)
    s = jnp.einsum('bsgrd,bcgd->bgrsc', q, kc) * ATTN_SCALE
    p = masked_softmax(s, cmp_end[None, :] <= t[:, None])
    o = jnp.einsum('bgrsc,bcgd->bsgrd', p.astype(vc.dtype), vc)
    return o, p

def selection_indices(p_cmp):
    S, n_cmp = p_cmp.shape[-2], p_cmp.shape[-1]
    n_sel = S // SEL_BLOCK
    c_start = jnp.arange(n_cmp) * CMP_STRIDE
    j = jnp.arange(n_sel)
    j_start = j * SEL_BLOCK
    overlap = jnp.clip(jnp.minimum(c_start[:, None] + CMP_BLOCK, j_start[None, :] + SEL_BLOCK)
                       - jnp.maximum(c_start[:, None], j_start[None, :]), 0, None)
    overlap = overlap.astype(jnp.float32) / CMP_BLOCK
    imp = jnp.einsum('bgrsc,cj->bgsj', p_cmp, overlap)
    t = jnp.arange(S)
    cur = t // SEL_BLOCK
    forced = (j[None, :] == 0) | (j[None, :] == cur[:, None]) | (j[None, :] == cur[:, None] - 1)
    imp = jnp.where(forced, FORCE, imp)
    imp = jnp.where(j_start[None, :] <= t[:, None], imp, NEG)
    _, idx = lax.top_k(imp, min(SEL_TOPN, n_sel))
    return idx.transpose(0, 2, 1, 3)

def selected_branch(q, ks, vs, sel_idx):
    B, S, G, R, Dh = q.shape
    n_sel = S // SEL_BLOCK
    n = sel_idx.shape[-1]
    k_blocks = ks.reshape(B, n_sel, SEL_BLOCK, G, Dh).transpose(0, 3, 1, 2, 4)
    v_blocks = vs.reshape(B, n_sel, SEL_BLOCK, G, Dh).transpose(0, 3, 1, 2, 4)
    b_ix = jnp.arange(B)[:, None, None, None]
    g_ix = jnp.arange(G)[None, None, :, None]

    def one_block(i):
        t0 = i * SEL_Q_BLOCK
        q_b = lax.dynamic_slice_in_dim(q, t0, SEL_Q_BLOCK, axis=1)
        idx_b = lax.dynamic_slice_in_dim(sel_idx, t0, SEL_Q_BLOCK, axis=1)
        k_sel = k_blocks[b_ix, g_ix, idx_b].reshape(B, SEL_Q_BLOCK, G, n * SEL_BLOCK, Dh)
        v_sel = v_blocks[b_ix, g_ix, idx_b].reshape(B, SEL_Q_BLOCK, G, n * SEL_BLOCK, Dh)
        kpos = (idx_b[..., None] * SEL_BLOCK + jnp.arange(SEL_BLOCK)).reshape(B, SEL_Q_BLOCK, G, n * SEL_BLOCK)
        t = t0 + jnp.arange(SEL_Q_BLOCK)
        mask = (kpos <= t[None, :, None, None])[:, :, :, None, :]
        s = jnp.einsum('btgrd,btgkd->btgrk', q_b, k_sel) * ATTN_SCALE
        p = masked_softmax(s, mask)
        return jnp.einsum('btgrk,btgkd->btgrd', p.astype(v_sel.dtype), v_sel)

    out = lax.map(one_block, jnp.arange(S // SEL_Q_BLOCK))
    return out.transpose(1, 0, 2, 3, 4, 5).reshape(B, S, G, R, Dh)

def window_branch(q, kw, vw):
    B, S, G, R, Dh = q.shape
    pad = ((0, 0), (WINDOW, 0), (0, 0), (0, 0))
    kp = jnp.pad(kw, pad)
    vp = jnp.pad(vw, pad)
    span = Q_BLOCK + WINDOW

    def one_block(i):
        t0 = i * Q_BLOCK
        q_b = lax.dynamic_slice_in_dim(q, t0, Q_BLOCK, axis=1)
        k_b = lax.dynamic_slice_in_dim(kp, t0, span, axis=1)
        v_b = lax.dynamic_slice_in_dim(vp, t0, span, axis=1)
        kpos = t0 - WINDOW + jnp.arange(span)
        t = t0 + jnp.arange(Q_BLOCK)
        diff = t[:, None] - kpos[None, :]
        mask = (diff >= 0) & (diff < WINDOW) & (kpos[None, :] >= 0)
        s = jnp.einsum('btgrd,bkgd->bgrtk', q_b, k_b) * ATTN_SCALE
        p = masked_softmax(s, mask)
        return jnp.einsum('bgrtk,bkgd->btgrd', p.astype(v_b.dtype), v_b)

    out = lax.map(one_block, jnp.arange(S // Q_BLOCK))
    return out.transpose(1, 0, 2, 3, 4, 5).reshape(B, S, G, R, Dh)

def dsa_branch(q, k, v, qi, ki, wi):
    B, S, G, R, Dh = q.shape
    topk = min(DSA_TOPK_MAX, S // 4)
    b_ix = jnp.arange(B)[:, None, None]
    key_pos = jnp.arange(S)
    wi = wi * (IDX_HEADS ** -0.5)

    def one_block(i):
        t0 = i * Q_BLOCK
        q_b = lax.dynamic_slice_in_dim(q, t0, Q_BLOCK, axis=1)
        qi_b = lax.dynamic_slice_in_dim(qi, t0, Q_BLOCK, axis=1)
        wi_b = lax.dynamic_slice_in_dim(wi, t0, Q_BLOCK, axis=1)
        t = t0 + jnp.arange(Q_BLOCK)
        logits = jnp.einsum('bthd,bsd->bths', qi_b, ki) * (IDX_DIM ** -0.5)
        score = jnp.einsum('bths,bth->bts', jax.nn.relu(logits), wi_b).astype(jnp.float32)
        score = jnp.where(key_pos[None, None, :] <= t[None, :, None], score, NEG)
        _, idx = lax.top_k(score, topk)
        k_sel = k[b_ix, idx]
        v_sel = v[b_ix, idx]
        mask = (idx <= t[None, :, None])[:, :, None, None, :]
        s = jnp.einsum('btgrd,btkgd->btgrk', q_b, k_sel) * ATTN_SCALE
        p = masked_softmax(s, mask)
        return jnp.einsum('btgrk,btkgd->btgrd', p.astype(v_sel.dtype), v_sel)

    out = lax.map(one_block, jnp.arange(S // Q_BLOCK))
    return out.transpose(1, 0, 2, 3, 4, 5).reshape(B, S, G, R, Dh)

def hybrid_layer(x, norm_gain, w_in, nsa_q_gain, nsa_kc_gain, nsa_ks_gain, nsa_kw_gain,
                 cmp_pe_k, cmp_k_w1, cmp_k_b1, cmp_k_w2, cmp_pe_v, cmp_v_w1, cmp_v_b1, cmp_v_w2,
                 dsa_q_gain, dsa_k_gain, w_out):
    B, S, _ = x.shape
    pos = jnp.arange(S, dtype=jnp.float32)
    h = rms_norm(x, norm_gain)
    proj = jnp.einsum('bsd,dc->bsc', h, w_in)
    (q_n, kc, vc, ks, vs, kw, vw, gate_logits, z_n,
     q_d, k_d, v_d, qi, ki, wi, z_d) = split_columns(proj, IN_WIDTHS)

    def heads(a, n):
        return a.reshape(B, S, n, HEAD_DIM)

    G, R = NSA_KV_HEADS, NSA_HEADS // NSA_KV_HEADS
    qn = rope(rms_norm(heads(q_n, NSA_HEADS), nsa_q_gain), pos).reshape(B, S, G, R, HEAD_DIM)
    kc_cmp = compress(heads(kc, G), cmp_pe_k, cmp_k_w1, cmp_k_b1, cmp_k_w2)
    vc_cmp = compress(heads(vc, G), cmp_pe_v, cmp_v_w1, cmp_v_b1, cmp_v_w2)
    cmp_pos = (jnp.arange(kc_cmp.shape[1]) * CMP_STRIDE + CMP_BLOCK - 1).astype(jnp.float32)
    kc_cmp = rope(rms_norm(kc_cmp, nsa_kc_gain), cmp_pos)
    o_cmp, p_cmp = compressed_branch(qn, kc_cmp, vc_cmp)
    sel_idx = selection_indices(p_cmp)
    ks_r = rope(rms_norm(heads(ks, G), nsa_ks_gain), pos)
    o_sel = selected_branch(qn, ks_r, heads(vs, G), sel_idx)
    kw_r = rope(rms_norm(heads(kw, G), nsa_kw_gain), pos)
    o_win = window_branch(qn, kw_r, heads(vw, G))
    g = jax.nn.sigmoid(gate_logits.astype(jnp.float32)).reshape(B, S, G, R, 3).astype(o_cmp.dtype)
    o_nsa = g[..., 0:1] * o_cmp + g[..., 1:2] * o_sel + g[..., 2:3] * o_win
    o_nsa = o_nsa.reshape(B, S, NSA_WIDTH) * jax.nn.silu(z_n)

    Gd, Rd = DSA_KV_HEADS, DSA_HEADS // DSA_KV_HEADS
    qd = rope(rms_norm(heads(q_d, DSA_HEADS), dsa_q_gain), pos).reshape(B, S, Gd, Rd, HEAD_DIM)
    kd = rope(rms_norm(heads(k_d, Gd), dsa_k_gain), pos)
    qi_r = rope(qi.reshape(B, S, IDX_HEADS, IDX_DIM), pos)
    ki_r = rope(ki.reshape(B, S, 1, IDX_DIM), pos).reshape(B, S, IDX_DIM)
    o_dsa = dsa_branch(qd, kd, heads(v_d, Gd), qi_r, ki_r, wi)
    o_dsa = o_dsa.reshape(B, S, DSA_WIDTH) * jax.nn.silu(z_d)

    mixed = jnp.concatenate([o_nsa, o_dsa], axis=-1)
    return x + jnp.einsum('bsc,cd->bsd', mixed, w_out)

def second_inputs(seed: int = 0) -> dict:
    key = jax.random.key(seed)
    k = jax.random.split(key, 18)
    L = DEPTH_2
    Dh = HEAD_DIM

    def nrm(kk, shape, scale):
        return jax.random.normal(kk, shape, jnp.float32) * scale

    def gain(kk, n):
        return 1.0 + 0.01 * jax.random.normal(kk, (L, n), jnp.float32)

    return {
        "x": nrm(k[0], (BATCH, SEQ, D_MODEL), 1.0),
        "norm_gain": gain(k[1], D_MODEL),
        "w_in": nrm(k[2], (L, D_MODEL, IN_COLS), D_MODEL ** -0.5),
        "nsa_q_gain": gain(k[3], Dh),
        "nsa_kc_gain": gain(k[4], Dh),
        "nsa_ks_gain": gain(k[5], Dh),
        "nsa_kw_gain": gain(k[6], Dh),
        "cmp_pe_k": nrm(k[7], (L, CMP_BLOCK, Dh), 0.1),
        "cmp_k_w1": nrm(k[8], (L, CMP_BLOCK * Dh, CMP_HIDDEN), (CMP_BLOCK * Dh) ** -0.5),
        "cmp_k_b1": nrm(k[9], (L, CMP_HIDDEN), 0.01),
        "cmp_k_w2": nrm(k[10], (L, CMP_HIDDEN, Dh), CMP_HIDDEN ** -0.5),
        "cmp_pe_v": nrm(k[11], (L, CMP_BLOCK, Dh), 0.1),
        "cmp_v_w1": nrm(k[12], (L, CMP_BLOCK * Dh, CMP_HIDDEN), (CMP_BLOCK * Dh) ** -0.5),
        "cmp_v_b1": nrm(k[13], (L, CMP_HIDDEN), 0.01),
        "cmp_v_w2": nrm(k[14], (L, CMP_HIDDEN, Dh), CMP_HIDDEN ** -0.5),
        "dsa_q_gain": gain(k[15], Dh),
        "dsa_k_gain": gain(k[16], Dh),
        "w_out": nrm(k[17], (L, MIX_WIDTH, D_MODEL), MIX_WIDTH ** -0.5),
    }

def second_block(x, norm_gain, w_in, nsa_q_gain, nsa_kc_gain, nsa_ks_gain, nsa_kw_gain,
              cmp_pe_k, cmp_k_w1, cmp_k_b1, cmp_k_w2, cmp_pe_v, cmp_v_w1, cmp_v_b1, cmp_v_w2,
              dsa_q_gain, dsa_k_gain, w_out):
    for l in range(DEPTH_2):
        x = hybrid_layer(x, norm_gain[l], w_in[l], nsa_q_gain[l], nsa_kc_gain[l], nsa_ks_gain[l],
                         nsa_kw_gain[l], cmp_pe_k[l], cmp_k_w1[l], cmp_k_b1[l], cmp_k_w2[l],
                         cmp_pe_v[l], cmp_v_w1[l], cmp_v_b1[l], cmp_v_w2[l],
                         dsa_q_gain[l], dsa_k_gain[l], w_out[l])
    return x


def setup_inputs(seed=0):
    out = dict(first_inputs(seed))
    for name, value in second_inputs(seed + 1).items():
        if name != "x":
            out[name + "_2"] = value
    return out


def reference(
    x, p, norm_mix, w_in_a, conv_a, w_out_a, w_in_b, conv_b, conv_bias_b, w_rgate_b, b_rgate_b,
    w_igate_b, b_igate_b, lam_b, w_out_b, norm_ffn, w_router_group, b_router_group,
    w_router_expert, b_router_expert, w_exp_gate, w_exp_up, w_exp_down, norm_ple, w_ple,
    w_ple_gate, b_ple_gate, norm_final, norm_gain_2, w_in_2, nsa_q_gain_2, nsa_kc_gain_2,
    nsa_ks_gain_2, nsa_kw_gain_2, cmp_pe_k_2, cmp_k_w1_2, cmp_k_b1_2, cmp_k_w2_2, cmp_pe_v_2,
    cmp_v_w1_2, cmp_v_b1_2, cmp_v_w2_2, dsa_q_gain_2, dsa_k_gain_2, w_out_2,
):
    x = first_block(
        x, p, norm_mix, w_in_a, conv_a, w_out_a, w_in_b, conv_b, conv_bias_b, w_rgate_b,
        b_rgate_b, w_igate_b, b_igate_b, lam_b, w_out_b, norm_ffn, w_router_group,
        b_router_group, w_router_expert, b_router_expert, w_exp_gate, w_exp_up, w_exp_down,
        norm_ple, w_ple, w_ple_gate, b_ple_gate, norm_final,
    )
    return second_block(
        x, norm_gain_2, w_in_2, nsa_q_gain_2, nsa_kc_gain_2, nsa_ks_gain_2, nsa_kw_gain_2,
        cmp_pe_k_2, cmp_k_w1_2, cmp_k_b1_2, cmp_k_w2_2, cmp_pe_v_2, cmp_v_w1_2, cmp_v_b1_2,
        cmp_v_w2_2, dsa_q_gain_2, dsa_k_gain_2, w_out_2,
    )


_drawn_inputs = setup_inputs


def setup_inputs(seed=0):
    import zlib

    import numpy as np

    out = dict(_drawn_inputs(seed))
    spreads = {}
    factors = {'b_rgate_b': 8.0,
     'b_igate_b': 8.0,
     'b_router_group': 5.059,
     'norm_ple': 3.431,
     'b_ple_gate': 8.0,
     'norm_gain_2': 8.0,
     'nsa_q_gain_2': 8.0,
     'nsa_kc_gain_2': 32.721,
     'nsa_ks_gain_2': 8.0,
     'nsa_kw_gain_2': 8.0,
     'cmp_pe_k_2': 8.0,
     'cmp_k_b1_2': 31.984,
     'cmp_pe_v_2': 16.018,
     'cmp_v_b1_2': 64.0,
     'dsa_q_gain_2': 8.0,
     'dsa_k_gain_2': 8.0}
    for name, (base, spread) in spreads.items():
        noise = np.random.default_rng([zlib.crc32(name.encode()), seed]).standard_normal(out[name].shape)
        drawn = base * np.exp(spread * noise) if base else spread * noise
        out[name] = __import__('jax').numpy.asarray(drawn.astype(out[name].dtype))
    for name, factor in factors.items():
        out[name] = (out[name] * factor).astype(out[name].dtype)
    return out
```

```python
from contextlib import ExitStack

import numpy as np

import concourse.bass as bass
from concourse import mybir

ALU = mybir.AluOpType
ACT = mybir.ActivationFunctionType
F32 = mybir.dt.float32
I32 = mybir.dt.int32
X = mybir.AxisListType.X

P = 128
S = 512
D = 1024
NT = S // P
KT = D // P
NE = 32
CAP = 64
NOVF = (2 * S) // (CAP + 1)
NB = NE + NOVF
RING = 5
UNIT = 4096
EPS = 1e-6
NEG = -1e30
SCALE = 0.125
NCMP = 31

CST = [
    ("ident", 128), ("tri", 128), ("strip", 512), ("ones", 128), ("cmpadd", 4 * NCMP), ("cmpmul", 4 * NCMP),
    ("cos", 4 * 32), ("sin", 4 * 32), ("ccos", 32), ("csin", 32),
    ("rev4", 4), ("rev8", 8), ("iota32", NE), ("iotab", NOVF), ("tok", NT),
    ("conva", 24), ("convb", 32), ("cbias", 8), ("br", 16), ("bi", 16), ("lam", 16),
    ("kb1", 2), ("vb1", 2), ("kpe", 16), ("vpe", 16), ("kw2", 128), ("vw2", 128),
    ("rw0", 8 * 36), ("rw1", 8 * 36), ("rb", 2 * 36),
]
OFF = {}
_o = 0
for _n, _w in CST:
    OFF[_n] = (_o, _o + _w)
    _o += _w
NCST = _o

ROWS = ["mix0", "ffn0", "ple0", "mix1", "ffn1", "ple1", "final", "att"]
HG = 22 * 64 + 128


class Core:

    def __init__(self, nc, ctx, tag, engines=("pe", "act", "dve", "pool", "sp")):
        self.sem = {e: ctx.enter_context(nc.semaphore(f"{tag}_{e}")) for e in engines}
        self.n = {e: 0 for e in engines}
        self.q = {e: [] for e in engines}
        self.seen = {e: {} for e in engines}

    def wait(self, eng, *toks):
        need = {}
        for sem, v in toks:
            if self.seen[eng].get(id(sem), 0) < v:
                need[id(sem)] = (sem, max(v, need.get(id(sem), (sem, 0))[1]))
        for k, (sem, v) in need.items():
            self.seen[eng][k] = v
            self.q[eng].append(lambda e, sem=sem, v=v: e.wait_ge(sem, v))

    def put(self, eng, fn, *toks, inc=True):
        self.wait(eng, *toks)
        if not inc:
            self.q[eng].append(fn)
            return None
        self.n[eng] += 1
        sem = self.sem[eng]
        self.q[eng].append(lambda e: fn(e).then_inc(sem, 1))
        return (sem, self.n[eng])

    def last(self, eng):
        return (self.sem[eng], self.n[eng])

    def pe(self, fn, *t, inc=True):
        return self.put("pe", fn, *t, inc=inc)

    def act(self, fn, *t):
        return self.put("act", fn, *t)

    def dve(self, fn, *t):
        return self.put("dve", fn, *t)

    def pool(self, fn, *t):
        return self.put("pool", fn, *t)


class Lane:

    def __init__(self, nc, ctx, name):
        self.sem = ctx.enter_context(nc.semaphore(name))
        self.n = 0

    def dma(self, core, eng, fn, *toks):
        core.wait(eng, *toks)
        self.n += 16
        core.q[eng].append(lambda e, s=self.sem: fn(e).then_inc(s, 16))
        return (self.sem, self.n)


def build(nc, t_):
    ctx = ExitStack()
    with ctx:
        def sb(name, shape, dt=F32):
            return ctx.enter_context(nc.sbuf_tensor(name, shape, dt))

        def dram(name, shape, dt=F32):
            return nc.dram_tensor(name, shape, dt, kind="Internal").ap()

        C = Core(nc, ctx, "m")
        ring = sb("ring", [P, RING * UNIT])
        h = sb("h", [P, NT, D])
        cst = sb("cst", [P, NCST])
        gbuf = sb("gbuf", [P, 2, D])
        small = sb("small", [P, 64])
        nspt = sb("nspt", [P, 16])
        zi = sb("zi", [P, NB], I32)
        AR = 23600
        arena = sb("arena", [P, AR])
        banks = [ctx.enter_context(nc.psum_tensor(f"ps{i}", [P, 512], F32)) for i in range(8)]
        bank_free = [[] for _ in range(8)]
        bank_at = [0]

        xs_d = [dram(f"xs_d{l}", [S, D]) for l in range(2)]
        slot_d = [dram(f"slot_d{l}", [CAP * NB, 1], I32) for l in range(2)]
        y_d = [dram(f"y_d{l}", [CAP * NB, D]) for l in range(2)]

        def cs(name):
            a, b = OFF[name]
            return cst[:, a:b]

        def ar(off, n):
            assert off + n <= AR, (off, n)
            return arena[:, off:off + n]

        def bank():
            b = bank_at[0]
            bank_at[0] = (b + 1) % 8
            return b

        ring_lane = [Lane(nc, ctx, f"ring{i}") for i in range(RING)]
        ring_free = {}
        ring_n = [0]

        class Unit:
            pass

        def load(src, width=UNIT):
            u = Unit()
            i = ring_n[0]
            ring_n[0] += 1
            u.i, s = i, i % RING
            u.ap = ring[:, s * UNIT:s * UNIT + width]
            u.tok = ring_lane[s].dma(C, "sp", lambda e, u=u: e.dma_start(u.ap, src), *(ring_free[i - RING] if i >= RING else []))
            return u

        def reserve():
            u = Unit()
            i = ring_n[0]
            ring_n[0] += 1
            u.i, s = i, i % RING
            u.ap = ring[:, s * UNIT:(s + 1) * UNIT]
            u.free = ring_free[i - RING]
            return u

        def release(u, *toks):
            ring_free[u.i] = list(toks)

        l_cst = Lane(nc, ctx, "l_cst")
        l_h = Lane(nc, ctx, "l_h")
        l_g = [Lane(nc, ctx, f"l_g{i}") for i in range(2)]
        g_tok = {}
        g_free = {}

        def load_gain(n):
            if n < len(ROWS):
                row = t_["rows"][n:n + 1, :].broadcast_to([P, D])
                g_tok[n] = l_g[n % 2].dma(C, "sp", lambda e, n=n, row=row: e.dma_start(gbuf[:, n % 2, :], row),
                                          *(g_free[n - 2] if n >= 2 else []))

        t_cst = l_cst.dma(C, "sp", lambda e: e.dma_start(cst[:], t_["cst"]))
        t_h = l_h.dma(C, "sp", lambda e: e.dma_start(h[:], t_["x"].rearrange("(t p) d -> p t d", p=P)))
        h_tok = [[t_h] for _ in range(NT)]
        load_gain(0)

        ident = cs("ident")
        ones = cs("ones")

        t = C.dve(lambda e: e.memset(zi[:], 0))
        l_z = Lane(nc, ctx, "l_z")
        tz = [l_z.dma(C, "pool", lambda e, l=l: e.dma_start(slot_d[l].rearrange("(s b) a -> s (b a)", b=NB), zi[0:CAP, :]), t) for l in range(2)]
        t_zero = tz[-1]

        def softplus_neg8():
            w = ar(0, 128)
            x_, a_, y_, z_, q_, s_ = (w[:, 16 * i:16 * i + 16] for i in range(6))
            lam = cs("lam")
            t = C.dve(lambda e: e.tensor_scalar(x_, lam, -1.0, None, ALU.mult), t_cst)
            t = C.dve(lambda e: e.tensor_tensor(a_, x_, lam, ALU.min), t)
            t = C.act(lambda e: e.activation(y_, a_, ACT.Exp), t)
            t = C.dve(lambda e: e.tensor_scalar(z_, y_, 2.0, None, ALU.add), t)
            t = C.dve(lambda e: e.reciprocal(z_, z_), t)
            t = C.dve(lambda e: e.tensor_tensor(z_, z_, y_, ALU.mult), t)
            t = C.dve(lambda e: e.tensor_tensor(q_, z_, z_, ALU.mult), t)
            t = C.dve(lambda e: e.tensor_scalar(s_, q_, 1.0 / 19, 1.0 / 17, ALU.mult, ALU.add), t)
            for n in (15, 13, 11, 9, 7, 5, 3, 1):
                t = C.dve(lambda e: e.tensor_tensor(s_, s_, q_, ALU.mult), t)
                t = C.dve(lambda e, n=n: e.tensor_scalar(s_, s_, 1.0 / n, None, ALU.add), t)
            t = C.dve(lambda e: e.tensor_tensor(s_, s_, z_, ALU.mult), t)
            t = C.dve(lambda e: e.tensor_scalar(x_, x_, 0.0, None, ALU.max), t)
            t = C.dve(lambda e: e.scalar_tensor_tensor(x_, s_, 2.0, x_, ALU.mult, ALU.add), t)
            return C.dve(lambda e: e.tensor_scalar(nspt[:], x_, -8.0, None, ALU.mult), t)

        tiny = small[:, 56:57]
        t_tiny = C.dve(lambda e: e.memset(tiny, 1e-30))
        t_nsp = softplus_neg8()
        arena_free = [t_nsp]
        safe = [arena_free]

        evac_at = [0]

        def evac(out, in_, *toks):
            evac_at[0] += 1
            if evac_at[0] % 2:
                return C.act(lambda e: e.activation(out, in_, ACT.Copy), *toks)
            return C.dve(lambda e: e.tensor_copy(out, in_), *toks)

        def norm_rows(n, dst, free, junk, also=None):
            out = []
            for i in range(NT):
                ss, rs = small[:, i:i + 1], small[:, 4 + i:5 + i]
                t = C.act(lambda e, i=i, ss=ss: e.activation(junk, h[:, i, :], ACT.Square, accum_out=ss), *h_tok[i], *safe[0])
                t = C.dve(lambda e, ss=ss, rs=rs: e.tensor_scalar(rs, ss, 1.0 / D, EPS, ALU.mult, ALU.add), t)
                t = C.act(lambda e, rs=rs: e.activation(rs, rs, ACT.Sqrt), t)
                t = C.dve(lambda e, rs=rs: e.reciprocal(rs, rs), t)
                t = C.dve(lambda e, i=i, rs=rs: e.scalar_tensor_tensor(dst(i), h[:, i, :], rs, gbuf[:, n % 2, :], ALU.mult, ALU.mult),
                          t, g_tok[n], *free(i), *safe[0])
                out.append(t)
                if also:
                    also(i, t)
            g_free[n] = [out[-1]]
            load_gain(n + 1)
            return out

        def transposed(xT, src, toks, i):
            done = []
            for hf in range(2):
                b = bank()
                for k in range(4):
                    kk = 4 * hf + k
                    t = C.pe(lambda e, b=b, k=k, kk=kk: e.transpose(banks[b][:, k * P:(k + 1) * P], src[:, kk * P:(kk + 1) * P], ident),
                             *(bank_free[b] if k == 0 else []), *toks, t_cst, inc=(k == 3))
                t = evac(xT[:, 4 * hf:4 * hf + 4, i * P:(i + 1) * P], banks[b][:].rearrange("p (k c) -> p k c", k=4), t)
                bank_free[b] = [t]
                done.append(t)
            return done, C.last("pe")

        def norm_T(n, xT, stage, junk, also=None):
            xs = stage.rearrange("p (b d) -> p b d", b=2)
            used = {}

            def free(i):
                return used.get(i - 2, [])

            res = []

            def after(i, t):
                extra = also(i, xs[:, i % 2, :], t) if also else []
                done, last = transposed(xT, xs[:, i % 2, :], [t], i)
                used[i] = [last, *extra]
                res.append(done)

            norm_rows(n, lambda i: xs[:, i % 2, :], free, junk, after)
            return res

        def mm_group(out_b, pairs, first, *toks, bias=None, width=512, rows=P):
            n = len(pairs)
            for j, (l, r) in enumerate(pairs):
                t = C.pe(lambda e, l=l, r=r, j=j: e.matmul(out_b, l, r, start=(j == 0), stop=(j == n - 1)),
                         *(toks if j == 0 else []), inc=(j == n - 1))
            return t

        def add_to_h(i, lo, n, b, t):
            t = C.dve(lambda e: e.tensor_tensor(h[:, i, lo:lo + n], h[:, i, lo:lo + n], banks[b][:, 0:n], ALU.add), t, *h_tok[i])
            bank_free[b] = [t]
            return t

        def out_proj(gT, g_toks, units):
            safe[0] = [C.last("pe"), C.last("act"), C.last("dve")]
            new = [[] for _ in range(NT)]
            for c, src in enumerate(units):
                u = load(src)
                w = u.ap.rearrange("p (k n) -> p k n", k=KT)
                for i in range(NT):
                    b = bank()
                    t = mm_group(banks[b][:], [(gT[:, k, i * P:(i + 1) * P], w[:, k, :]) for k in range(KT)], True,
                                 u.tok, *bank_free[b], *g_toks)
                    tt = add_to_h(i, 512 * c, 512, b, t)
                    new[i].append(tt)
                release(u, t)
            for i in range(NT):
                h_tok[i] = [max(new[i], key=lambda z: z[1])]

        W = t_["wall"]
        wat = [0]

        def wnext():
            wat[0] += 1
            return W[wat[0] - 1]

        l_cy = [Lane(nc, ctx, f"l_cy{l}") for l in range(2)]
        cy_t = []

        def clear_y():
            z = ar(AR - D, D)
            t = C.dve(lambda e: e.memset(z, 0.0))
            for l in range(2):
                cy_t.append(l_cy[l].dma(C, "sp", lambda e, l=l: e.dma_start(
                    y_d[l].rearrange("(s b) d -> s b d", b=NB)[:, NE:, :], z[0:CAP, :].unsqueeze(1).broadcast_to([CAP, NOVF, D])), t))

        def mixer_a():
            xT = ar(0, 4096).rearrange("p (k s) -> p k s", k=KT)
            gT = ar(4096, 4096).rearrange("p (k s) -> p k s", k=KT)
            res = norm_T(0, xT, ar(8192, 2048), ar(10240, 1024))
            xt = [t for r in res for t in r]
            cS = ar(11264, 1024).rearrange("p (b s) -> p b s", b=2)
            v = ar(12288, 1028).rearrange("p (b s) -> p b s", b=2)
            u1 = ar(13316, 1024).rearrange("p (b s) -> p b s", b=2)
            tz = C.dve(lambda e: e.memset(v, 0.0), *arena_free)
            ca = cs("conva").rearrange("p (c k) -> p c k", c=8)
            freec, gt = {}, []
            for q in range(2):
                us = [load(wnext()) for _ in range(3)]
                if q == 1:
                    clear_y()
                for c4 in range(4):
                    c = 4 * q + c4
                    bs, ts = [], []
                    for u in us:
                        b = bank()
                        w = u.ap.rearrange("p (k n) -> p k n", k=KT)
                        ts.append(mm_group(banks[b][:], [(w[:, k, c4 * P:(c4 + 1) * P], xT[:, k, :]) for k in range(KT)], True,
                                           u.tok, *bank_free[b], *xt))
                        bs.append(b)
                        if c4 == 3:
                            release(u, ts[-1])
                    j = c % 2
                    t1 = C.act(lambda e, j=j, b=bs[1]: e.activation(cS[:, j, :], banks[b][:], ACT.Copy), ts[1], *freec.get(c - 2, []))
                    bank_free[bs[1]] = [t1]
                    t = C.dve(lambda e, j=j, b=bs[2]: e.tensor_tensor(v[:, j, 1:513], cS[:, j, :], banks[b][:], ALU.mult),
                              t1, ts[2], tz, *freec.get(c - 2, []))
                    bank_free[bs[2]] = [t]
                    t = C.act(lambda e, j=j, c=c: e.activation(u1[:, j, :], v[:, j, 0:512], ACT.Copy, scale=ca[:, c, 0:1]), t, *freec.get(c - 2, []))
                    t = C.dve(lambda e, j=j, c=c: e.scalar_tensor_tensor(u1[:, j, :], v[:, j, 1:513], ca[:, c, 1:2], u1[:, j, :], ALU.mult, ALU.add), t)
                    t = C.dve(lambda e, j=j, c=c: e.scalar_tensor_tensor(u1[:, j, :], v[:, j, 2:514], ca[:, c, 2:3], u1[:, j, :], ALU.mult, ALU.add), t)
                    t = C.dve(lambda e, j=j, c=c, b=bs[0]: e.tensor_tensor(gT[:, c, :], u1[:, j, :], banks[b][:], ALU.mult), t, ts[0])
                    bank_free[bs[0]] = [t]
                    freec[c] = [t]
                    gt = [t]
            out_proj(gT, gt, [wnext(), wnext()])

        def moe(l):
            n = 1 + 3 * l
            xT = ar(0, 4096).rearrange("p (k s) -> p k s", k=KT)
            l_xs = [Lane(nc, ctx, f"l_xs{l}_{i}") for i in range(NT)]
            xs_t = []

            def store(i, src, t):
                xs_t.append(l_xs[i].dma(C, "pool", lambda e: e.dma_start(xs_d[l][i * P:(i + 1) * P, :], src), t))
                return [xs_t[-1]]

            res = norm_T(n, xT, ar(8192, 2048), ar(10240, 1024), store)
            lg = ar(11264, 144).rearrange("p (t e) -> p t e", t=NT)
            rw = cs(f"rw{l}").rearrange("p (k e) -> p k e", k=KT)
            rb = cs("rb")[0:1, l * 36:(l + 1) * 36]
            b = bank()
            for i in range(NT):
                o = banks[b][:, i * 36:(i + 1) * 36]
                t = C.pe(lambda e, o=o: e.matmul(o, ones[0:1, :], rb, start=True, stop=False), *bank_free[b], *res[i], inc=False)
                for k in range(KT):
                    t = C.pe(lambda e, k=k, o=o, i=i: e.matmul(o, xT[:, k, i * P:(i + 1) * P], rw[:, k, :], start=False, stop=(k == 7)), inc=(k == 7))
            t = C.dve(lambda e, b=b: e.tensor_copy(ar(11264, 144), banks[b][:, 0:144]), t)
            bank_free[b] = [t]
            G = lg[:, :, 0:4]
            L = lg[:, :, 4:36].rearrange("p t (g e) -> p t g e", g=4)
            so = [11520]

            def alloc(*dims):
                w = int(np.prod(dims))
                a = ar(so[0], w)
                so[0] += w
                if len(dims) == 2:
                    a = a.rearrange("p (a b) -> p a b", a=dims[0])
                if len(dims) == 3:
                    a = a.rearrange("p (a b c) -> p a b c", a=dims[0], b=dims[1])
                return a

            def TT(out, a, b_, op, *tk):
                return C.dve(lambda e: e.tensor_tensor(out, a, b_, op), *tk)

            def RD(out, a, op, *tk):
                return C.dve(lambda e: e.tensor_reduce(out, a, X, op), *tk)

            def TS(out, a, s1, op, *tk, s2=None, op2=None):
                if op2 is None:
                    return C.dve(lambda e: e.tensor_scalar(out, a, s1, None, op), *tk)
                return C.dve(lambda e: e.tensor_scalar(out, a, s1, s2, op, op2), *tk)

            gm = alloc(4)
            t = RD(gm, G, ALU.max, t)
            eg = alloc(4, 4)
            gmb = gm.unsqueeze(2).broadcast_to([P, 4, 4])
            t = TT(eg, G, gmb, ALU.subtract, t)
            cand = alloc(4, 4)
            tc = TS(cand, eg, 0.0, ALU.is_equal, t)
            t_e = C.act(lambda e: e.activation(eg, eg, ACT.Exp), tc)
            rev4 = cs("rev4").unsqueeze(1).broadcast_to([P, 4, 4])
            t = TT(cand, cand, rev4, ALU.mult, tc)
            g1 = alloc(4)
            t = RD(g1, cand, ALU.max, t)
            ohg = alloc(4, 4)
            t = TT(ohg, rev4, g1.unsqueeze(2).broadcast_to([P, 4, 4]), ALU.is_equal, t)
            ohgb = ohg.unsqueeze(3).broadcast_to([P, 4, 4, 8])
            ml = alloc(4, 4, 8)
            t = TT(ml, L, ohgb, ALU.mult, t)
            ls = alloc(4, 8)
            t = RD(ls, ml.rearrange("p t g e -> p t e g"), ALU.add, t)
            rev8 = cs("rev8").unsqueeze(1).broadcast_to([P, 4, 8])
            ms, ohs = [], []
            for r in range(2):
                m = alloc(4)
                t = RD(m, ls, ALU.max, t)
                c8 = alloc(4, 8)
                t = TT(c8, ls, m.unsqueeze(2).broadcast_to([P, 4, 8]), ALU.is_equal, t)
                t = TT(c8, c8, rev8, ALU.mult, t)
                i1 = alloc(4)
                t = RD(i1, c8, ALU.max, t)
                oh = alloc(4, 8)
                t = TT(oh, rev8, i1.unsqueeze(2).broadcast_to([P, 4, 8]), ALU.is_equal, t)
                if r == 0:
                    t = C.dve(lambda e, oh=oh: e.scalar_tensor_tensor(ls, oh, -1e38, ls, ALU.mult, ALU.add), t)
                ms.append(m)
                ohs.append(oh)
            sg = alloc(4)
            t = RD(sg, eg, ALU.add, t, t_e)
            d2 = alloc(4)
            t = TT(d2, ms[1], ms[0], ALU.subtract, t)
            t = C.act(lambda e: e.activation(d2, d2, ACT.Exp), t)
            q2 = alloc(4)
            t = TS(q2, d2, 1.0, ALU.add, t)
            t = TT(q2, q2, sg, ALU.mult, t)
            wt = small[:, 8 + 8 * l:16 + 8 * l]
            t = C.dve(lambda e: e.reciprocal(wt[:, 0:4], q2), t)
            t = TT(wt[:, 4:8], wt[:, 0:4], d2, ALU.mult, t)
            OH = []
            for r in range(2):
                o = alloc(4, 4, 8)
                t = TT(o, ohgb, ohs[r].unsqueeze(2).broadcast_to([P, 4, 4, 8]), ALU.mult, t)
                OH.append(o)
            oh = alloc(4, 4, 8)
            t = TT(oh, OH[0], OH[1], ALU.add, t)
            ohf = oh.rearrange("p t g e -> p t (g e)")
            b = bank()
            for i in range(NT):
                o = banks[b][:, 32 * i:32 * i + 32]
                for j in range(i + 1):
                    C.pe(lambda e, o=o, i=i, j=j: e.matmul(o, cs("tri") if j == i else ones, ohf[:, j, :], start=(j == 0), stop=(j == i)),
                         t, *bank_free[b], inc=False)
            for j in range(NT):
                tp = C.pe(lambda e, j=j: e.matmul(banks[b][:, 128:160], ones, ohf[:, j, :], start=(j == 0), stop=(j == 3)), inc=(j == 3))
            rc = alloc(160)
            t = C.dve(lambda e: e.tensor_copy(rc, banks[b][:, 0:160]), tp)
            bank_free[b] = [t]
            rk = rc[:, 0:128]
            cnt = rc[:, 128:160]
            nx = alloc(32)
            t = TS(nx, cnt, float(CAP), ALU.is_gt, t)
            tmp32 = alloc(32)
            for j in range(2, S // CAP):
                t = TS(tmp32, cnt, float(j * CAP), ALU.is_gt, t)
                t = TT(nx, nx, tmp32, ALU.add, t)
            cum = alloc(32)
            one32 = ones[:, 0:32]
            t = C.dve(lambda e: e.tensor_tensor_scan(cum, one32, nx, 0.0, ALU.mult, ALU.add), t)
            base = alloc(32)
            t = TT(base, cum, nx, ALU.subtract, t)
            t = TT(base, base, cs("iota32"), ALU.subtract, t)
            t = TS(base, base, 31.0, ALU.add, t)
            q = alloc(128)
            t = TS(q, rk, float(CAP), ALU.is_ge, t)
            ex = alloc(4, 32)
            t = TT(ex, q.rearrange("p (t e) -> p t e", t=4), base.unsqueeze(1).broadcast_to([P, 4, 32]), ALU.mult, t)
            t = TT(ex, ex, cs("iota32").unsqueeze(1).broadcast_to([P, 4, 32]), ALU.add, t)
            tq = alloc(128)
            for j in range(2, S // CAP):
                t = TS(tq, rk, float(j * CAP), ALU.is_ge, t)
                t = TT(q, q, tq, ALU.add, t)
            pf = alloc(128)
            t = C.dve(lambda e: e.scalar_tensor_tensor(pf, rk, float(NB), ex.rearrange("p t e -> p (t e)"), ALU.mult, ALU.add), t)
            t = C.dve(lambda e: e.scalar_tensor_tensor(pf, q, float(1 - CAP * NB), pf, ALU.mult, ALU.add), t)
            pos_i = posi[l]
            for r in range(2):
                mp = alloc(4, 32)
                t = TT(mp, OH[r].rearrange("p t g e -> p t (g e)"), pf.rearrange("p (t e) -> p t e", t=4), ALU.mult, t)
                pr = alloc(4)
                t = RD(pr, mp, ALU.add, t)
                t = C.dve(lambda e, r=r, pr=pr: e.tensor_copy(pos_i[:, 4 * r:4 * r + 4], pr), t)
            t_pos = t
            cmpb = alloc(NOVF, 32)
            t = TT(cmpb, cum.unsqueeze(1).broadcast_to([P, NOVF, 32]), cs("iotab").unsqueeze(2).broadcast_to([P, NOVF, 32]), ALU.is_le, t)
            eo = alloc(NOVF)
            t = RD(eo, cmpb, ALU.add, t)
            t = TS(eo, eo, float(NE - 1), ALU.min, t)
            C.dve(lambda e: e.tensor_copy(ovf_i[l][:, 0:NOVF], eo), t)
            t_ovf = C.dve(lambda e: e.tensor_copy(ovf_i[l][:, NOVF:NOVF + 1], cum[:, 31:32]), t)
            assert so[0] <= AR

            l_sc = Lane(nc, ctx, f"l_sc{l}")
            tsc = None
            for r in range(2):
                for i in range(NT):
                    tsc = l_sc.dma(C, "pool", lambda e, r=r, i=i: e.indirect_dma_start(
                        out=slot_d[l], out_offset=bass.IndirectOffsetOnAxis(ap=pos_i[:, 4 * r + i:4 * r + i + 1], axis=0),
                        in_=toki[:, i:i + 1], in_offset=None), t_pos, t_zero, t_toki, *([tsc] if tsc else []))
            l_ix = Lane(nc, ctx, f"l_ix{l}")
            t_ix = l_ix.dma(C, "pool", lambda e: e.dma_start(idx[0:CAP, :], slot_d[l].rearrange("(s b) a -> s (b a)", b=NB)), tsc)

            o = 0
            xe = ar(o, 3072).rearrange("p (b d) -> p b d", b=3)
            xeT = ar(o + 3072, 2 * KT * CAP).rearrange("p (b k c) -> p b k c", b=2, k=KT)
            o += 3072 + 2 * KT * CAP
            sl = ar(o, 1024).rearrange("p (b d) -> p b d", b=2)
            hh = ar(o + 1024, 1024).rearrange("p (b d) -> p b d", b=2)
            hT = ar(o + 2048, 2 * 4 * CAP).rearrange("p (b k c) -> p b k c", b=2, k=4)
            o += 2048 + 8 * CAP
            yy = ar(o, 2048).rearrange("p (b d) -> p b d", b=2)
            o += 2048
            l_ge = [Lane(nc, ctx, f"l_ge{l}_{i}") for i in range(3)]
            l_ys = [Lane(nc, ctx, f"l_ys{l}_{i}") for i in range(2)]
            entry = [C.last("pe"), C.last("dve"), C.last("act")]
            ge_t, xT_t, free_xe, free_xeT = {}, {}, {}, {}
            hh_t, hT_t, free_hh, free_hT, free_sl, y_free, ys_t = {}, {}, {}, {}, {}, {}, {}

            def gather(e_):
                j = e_ % 3
                ge_t[e_] = l_ge[j].dma(C, "pool", lambda e: e.indirect_dma_start(
                    out=xe[0:CAP, j, :], out_offset=None, in_=xs_d[l],
                    in_offset=bass.IndirectOffsetOnAxis(ap=idx[0:CAP, e_:e_ + 1], axis=0)),
                    t_ix, *xs_t, *entry, *free_xe.get(e_ - 3, []))

            def XT(e_):
                j = e_ % 2
                nb = KT * CAP // 512
                done = []
                for q_ in range(nb):
                    b = bank()
                    per = 512 // CAP
                    for k in range(per):
                        kk = q_ * per + k
                        t = C.pe(lambda e, b=b, k=k, kk=kk: e.transpose(banks[b][:, k * CAP:(k + 1) * CAP], xe[0:CAP, e_ % 3, kk * P:(kk + 1) * P], ident[0:CAP, 0:CAP]),
                                 ge_t[e_], *bank_free[b], inc=(k == per - 1))
                    tt = C.dve(lambda e, b=b, q_=q_: e.tensor_copy(xeT[:, j, q_ * per:(q_ + 1) * per, :], banks[b][:].rearrange("p (k c) -> p k c", k=per)),
                               t, *free_xeT.get(e_ - 2, []), *entry)
                    bank_free[b] = [tt]
                    done.append(tt)
                free_xe[e_] = [t]
                xT_t[e_] = done

            def GU(e_, core=C):
                j = e_ % 2
                us = [load(t_["wexp"][l, e_, m_]) for m_ in range(2)]
                ws = [u.ap.rearrange("p (k n) -> p k n", k=KT) for u in us]
                bs = [bank(), bank()]
                outs = [banks[bs[0]][0:CAP, :], banks[bs[1]][64:64 + CAP, :]]
                for k in range(KT):
                    for m_ in range(2):
                        t = C.pe(lambda e, k=k, m_=m_: e.matmul(outs[m_], xeT[:, j, k, :], ws[m_][:, k, :], start=(k == 0), stop=(k == KT - 1)),
                                 us[m_].tok, *bank_free[bs[m_]], *xT_t[e_], inc=(k == KT - 1 and m_ == 1))
                ts = [t, t]
                for u in us:
                    release(u, t)
                free_xeT[e_] = [ts[1]]
                t = C.act(lambda e: e.activation(sl[0:CAP, j, :], banks[bs[0]][0:CAP, :], ACT.Silu), ts[0], *free_sl.get(e_ - 2, []), *entry)
                bank_free[bs[0]] = [t]
                t = C.dve(lambda e: e.tensor_tensor(hh[0:CAP, j, :], sl[0:CAP, j, :], banks[bs[1]][64:64 + CAP, :], ALU.mult), t, ts[1], *free_hh.get(e_ - 2, []))
                bank_free[bs[1]] = [t]
                free_sl[e_] = [t]
                hh_t[e_] = t

            def HT(e_):
                j = e_ % 2
                b = bank()
                for k in range(4):
                    t = C.pe(lambda e, k=k: e.transpose(banks[b][:, k * CAP:(k + 1) * CAP], hh[0:CAP, j, k * P:(k + 1) * P], ident[0:CAP, 0:CAP]),
                             hh_t[e_], *bank_free[b], inc=(k == 3))
                free_hh[e_] = [t]
                t = C.act(lambda e: e.activation(hT[:, j, :, :], banks[b][:, 0:4 * CAP].rearrange("p (k c) -> p k c", k=4), ACT.Copy),
                          t, *free_hT.get(e_ - 2, []), *entry)
                bank_free[b] = [t]
                hT_t[e_] = t

            def DOWN(e_):
                j = e_ % 2
                u = load(t_["wexp"][l, e_, 2])
                w = u.ap.rearrange("p (k n) -> p k n", k=4)
                bs = [bank(), bank()]
                outs = [banks[bs[0]][0:CAP, :], banks[bs[1]][64:64 + CAP, :]]
                for k in range(4):
                    for c in range(2):
                        t = C.pe(lambda e, k=k, c=c: e.matmul(outs[c], hT[:, j, k, :], w[:, k, c * 512:(c + 1) * 512], start=(k == 0), stop=(k == 3)),
                                 u.tok, *bank_free[bs[c]], hT_t[e_], inc=(k == 3 and c == 1))
                ta = C.act(lambda e: e.activation(yy[0:CAP, j, 0:512], outs[0], ACT.Copy), t, *y_free.get(e_ - 2, []), *entry)
                tb = C.dve(lambda e: e.tensor_copy(yy[0:CAP, j, 512:1024], outs[1]), t, *y_free.get(e_ - 2, []), *entry)
                bank_free[bs[0]], bank_free[bs[1]] = [ta], [tb]
                out = [ta, tb]
                release(u, t)
                free_hT[e_] = [t]
                ys_t[e_] = l_ys[j].dma(C, "pool", lambda e: e.dma_start(y_d[l].rearrange("(s b) d -> b s d", b=NB)[e_], yy[0:CAP, j, :]), *out)
                y_free[e_] = [ys_t[e_]]

            gather(0)
            gather(1)
            XT(0)
            for e_ in range(NE):
                if e_ + 2 < NE:
                    gather(e_ + 2)
                GU(e_)
                if e_ >= 1:
                    DOWN(e_ - 1)
                if e_ + 1 < NE:
                    XT(e_ + 1)
                HT(e_)
            DOWN(NE - 1)

            main = [cy_t[l], C.last("pe"), C.last("act"), C.last("dve"), ys_t[NE - 1], ys_t[NE - 2], t_ovf]
            O = Core(nc, ctx, f"o{l}", engines=("pe", "act", "dve"))
            lw = Lane(nc, ctx, f"lw{l}")
            lo = Lane(nc, ctx, f"lo{l}")
            lists = {e: [] for e in C.q}
            prev = []
            for bk in range(NOVF):
                q0 = {e: [] for e in C.q}
                O.q = q0
                O.seen = {e: {} for e in C.q}
                for e in C.q:
                    O.wait(e, *main, *prev)
                for m_ in range(3):
                    tw = lw.dma(O, "sp", lambda e, m_=m_: e.dma_start(ring[:, m_ * UNIT:(m_ + 1) * UNIT], t_["wexp"][l, bass.DynSlice(eo_box[0], 1), m_].rearrange("a p n -> (a p) n")))
                tg = lo.dma(O, "pool", lambda e, bk=bk: e.indirect_dma_start(
                    out=xe[0:CAP, 0, :], out_offset=None, in_=xs_d[l],
                    in_offset=bass.IndirectOffsetOnAxis(ap=idx[0:CAP, NE + bk:NE + bk + 1], axis=0)))
                ev = []
                for q_ in range(KT * CAP // 512):
                    per = 512 // CAP
                    for k in range(per):
                        kk = q_ * per + k
                        t = O.pe(lambda e, q_=q_, k=k, kk=kk: e.transpose(banks[q_][:, k * CAP:(k + 1) * CAP], xe[0:CAP, 0, kk * P:(kk + 1) * P], ident[0:CAP, 0:CAP]), tg)
                    ev.append(O.dve(lambda e, q_=q_, per=per: e.tensor_copy(xeT[:, 0, q_ * per:(q_ + 1) * per, :], banks[q_][:].rearrange("p (k c) -> p k c", k=per)), t))
                for m_ in range(2):
                    w = ring[:, m_ * UNIT:(m_ + 1) * UNIT].rearrange("p (k n) -> p k n", k=KT)
                    for k in range(KT):
                        t = O.pe(lambda e, m_=m_, k=k, w=w: e.matmul(banks[2 + m_][0:CAP, :], xeT[:, 0, k, :], w[:, k, :], start=(k == 0), stop=(k == 7)), tw, *ev)
                t = O.act(lambda e: e.activation(sl[0:CAP, 0, :], banks[2][0:CAP, :], ACT.Silu), t)
                t = O.dve(lambda e: e.tensor_tensor(hh[0:CAP, 0, :], sl[0:CAP, 0, :], banks[3][0:CAP, :], ALU.mult), t)
                for k in range(4):
                    t2 = O.pe(lambda e, k=k: e.transpose(banks[4][:, k * CAP:(k + 1) * CAP], hh[0:CAP, 0, k * P:(k + 1) * P], ident[0:CAP, 0:CAP]), t)
                t = O.act(lambda e: e.activation(hT[:, 0, :, :], banks[4][:, 0:4 * CAP].rearrange("p (k c) -> p k c", k=4), ACT.Copy), t2)
                w = ring[:, 2 * UNIT:3 * UNIT].rearrange("p (k n) -> p k n", k=4)
                for c in range(2):
                    for k in range(4):
                        t3 = O.pe(lambda e, c=c, k=k, w=w: e.matmul(banks[5 + c][0:CAP, :], hT[:, 0, k, :], w[:, k, c * 512:(c + 1) * 512], start=(k == 0), stop=(k == 3)), t)
                ta = O.act(lambda e: e.activation(yy[0:CAP, 0, 0:512], banks[5][0:CAP, :], ACT.Copy), t3)
                tb = O.dve(lambda e: e.tensor_copy(yy[0:CAP, 0, 512:1024], banks[6][0:CAP, :]), t3)
                ty = lo.dma(O, "pool", lambda e, bk=bk: e.dma_start(y_d[l].rearrange("(s b) d -> b s d", b=NB)[NE + bk], yy[0:CAP, 0, :]), ta, tb)
                for e in C.q:
                    O.wait(e, ty)
                    lists[e].append(q0[e])
                prev = [ty]

            def emit(e, steps, name, l=l):
                nv = e.value_load(ovf_i[l][0:1, NOVF:NOVF + 1], min_val=0, max_val=NOVF)

                def rec(bk):
                    if bk == len(steps):
                        return
                    with e.If(nv > bk):
                        if name == "sp":
                            eo_box[0] = e.value_load(ovf_i[l][0:1, bk:bk + 1], min_val=0, max_val=NE - 1)
                        for f in steps[bk]:
                            f(e)
                        rec(bk + 1)
                rec(0)

            for e in C.q:
                C.wait(e, t_ovf)
                C.q[e].append(lambda en, e=e: emit(en, lists[e], e))

            yg = ar(12288, 8192).rearrange("p (b d) -> p b d", b=8)
            l_yg = [Lane(nc, ctx, f"l_yg{l}_{i}") for i in range(8)]
            for i in range(NT):
                tk = []
                for r in range(2):
                    j = 2 * i + r
                    tk.append(l_yg[j].dma(C, "pool", lambda e, i=i, r=r, j=j: e.indirect_dma_start(
                        out=yg[:, j, :], out_offset=None, in_=y_d[l],
                        in_offset=bass.IndirectOffsetOnAxis(ap=pos_i[:, 4 * r + i:4 * r + i + 1], axis=0)),
                        ys_t[NE - 1], ys_t[NE - 2], cy_t[l], C.last("dve"), C.last("act")))
                for r in range(2):
                    j = 2 * i + r
                    t = C.dve(lambda e, i=i, r=r, j=j: e.scalar_tensor_tensor(
                        h[:, i, :], yg[:, j, :], wt[:, 4 * r + i:4 * r + i + 1], h[:, i, :], ALU.mult, ALU.add), tk[r], *h_tok[i])
                    h_tok[i] = [t]

        eo_box = [None]
        posi = [sb(f"posi{l}", [P, 8], I32) for l in range(2)]
        ovf_i = [sb(f"ovfi{l}", [P, NOVF + 1], I32) for l in range(2)]
        toki = sb("toki", [P, NT], I32)
        idx = sb("idx", [P, NB], I32)
        t_toki = C.dve(lambda e: e.tensor_copy(toki[:], cs("tok")), t_cst)

        l_p = [Lane(nc, ctx, f"l_p{l}") for l in range(2)]

        def ple(l):
            n = 2 + 3 * l
            xT = ar(0, 4096).rearrange("p (k s) -> p k s", k=KT)
            pT = ar(7168, 1024).rearrange("p (k s) -> p k s", k=2)
            br = ar(8192, 1024)
            entry = [C.last("pe"), C.last("dve"), C.last("act")]
            res = norm_T(n, xT, ar(4096, 2048), ar(6144, 1024))
            t_p = l_p[l].dma(C, "pool", lambda e: e.dma_start(ar(7168, 1024), t_["pT"][l]), *entry)
            t_p = l_p[l].dma(C, "pool", lambda e: e.dma_start(br[0:1, :], t_["plebias"][l:l + 1, :]), *entry)
            up = load(wnext()[:, 0:2048], 2048)
            wp = up.ap.rearrange("p (k n) -> p k n", k=2)
            sg = ar(9216, 1024).rearrange("p (b s) -> p b s", b=2)
            fr = {}
            new = [[] for _ in range(NT)]
            c_ = 0
            for c in range(2):
                u = load(wnext())
                w = u.ap.rearrange("p (k n) -> p k n", k=KT)
                for i in range(NT):
                    j = c_ % 2
                    b = bank()
                    C.pe(lambda e, b=b, c=c: e.matmul(banks[b][:], ones[0:1, :], br[0:1, 512 * c:512 * c + 512], start=True, stop=False),
                         t_p, *bank_free[b], inc=False)
                    for k in range(KT):
                        t = C.pe(lambda e, b=b, k=k, i=i, w=w: e.matmul(banks[b][:], xT[:, k, i * P:(i + 1) * P], w[:, k, :], start=False, stop=(k == 7)),
                                 u.tok, *res[i], inc=(k == 7))
                    b2 = bank()
                    t2 = mm_group(banks[b2][:], [(pT[:, k, i * P:(i + 1) * P], wp[:, k, 512 * c:512 * c + 512]) for k in range(2)], True,
                                  up.tok, *bank_free[b2])
                    t = C.act(lambda e, b=b, j=j: e.activation(sg[:, j, :], banks[b][:], ACT.Sigmoid), t, *fr.get(c_ - 2, []), *entry)
                    bank_free[b] = [t]
                    t = C.dve(lambda e, b2=b2, j=j: e.tensor_tensor(sg[:, j, :], sg[:, j, :], banks[b2][:], ALU.mult), t, t2)
                    bank_free[b2] = [t]
                    t = C.dve(lambda e, i=i, c=c, j=j: e.tensor_tensor(h[:, i, 512 * c:512 * c + 512], h[:, i, 512 * c:512 * c + 512], sg[:, j, :], ALU.add), t, *h_tok[i])
                    fr[c_] = [t]
                    new[i].append(t)
                    c_ += 1
                release(u, C.last("pe"))
                if c == 1:
                    release(up, C.last("pe"))
            for i in range(NT):
                h_tok[i] = [new[i][-1]]

        def mixer_b():
            xT = ar(0, 4096).rearrange("p (k s) -> p k s", k=KT)
            yT = ar(4096, 4096).rearrange("p (k s) -> p k s", k=KT)
            uc = ar(8192, 4096).rearrange("p (k s) -> p k s", k=KT)
            hs = ar(12288, 4096).rearrange("p (k s) -> p k s", k=KT)
            entry = [C.last("pe"), C.last("dve"), C.last("act"), *cy_t]
            res = norm_T(3, xT, ar(16384, 2048), ar(18432, 1024))
            xt = [t for r in res for t in r]
            up = ar(22528, 1032).rearrange("p (b s) -> p b s", b=2)
            tz = C.dve(lambda e: e.memset(up, 0.0), *entry)
            cb = cs("convb").rearrange("p (c k) -> p c k", c=8)
            fr, uct, yt = {}, {}, {}
            for q in range(4):
                u = load(wnext())
                w = u.ap.rearrange("p (k n) -> p k n", k=KT)
                for c4 in range(4):
                    b = bank()
                    t = mm_group(banks[b][:], [(w[:, k, c4 * P:(c4 + 1) * P], xT[:, k, :]) for k in range(KT)], True,
                                 u.tok, *bank_free[b], *xt)
                    c = 4 * (q % 2) + c4
                    if q >= 2:
                        t = C.act(lambda e, b=b, c=c: e.activation(yT[:, c, :], banks[b][:], ACT.Gelu_apprx_tanh), t, *entry)
                        bank_free[b] = [t]
                        yt[c] = t
                    else:
                        j = c % 2
                        t = C.act(lambda e, b=b, j=j: e.activation(up[:, j, 2:514], banks[b][:], ACT.Copy), t, tz, *fr.get(c - 2, []))
                        bank_free[b] = [t]
                        t = C.dve(lambda e, j=j, c=c: e.tensor_scalar(uc[:, c, :], up[:, j, 0:512], cb[:, c, 0:1], cs("cbias")[:, c:c + 1], ALU.mult, ALU.add), t, *entry)
                        for m in range(1, 4):
                            t = C.dve(lambda e, j=j, c=c, m=m: e.scalar_tensor_tensor(uc[:, c, :], up[:, j, m:m + 512], cb[:, c, m:m + 1], uc[:, c, :], ALU.mult, ALU.add), t)
                        fr[c] = [t]
                        uct[c] = t
                release(u, C.last("pe"))
            R_ = ar(16384, 2048).rearrange("p (k s) -> p k s", k=4)
            I_ = ar(18432, 2048).rearrange("p (k s) -> p k s", k=4)
            T_ = ar(20480, 2048).rearrange("p (k s) -> p k s", k=4)
            fr = [C.last("dve"), C.last("pe")]
            hst = {}
            for d in range(2):
                u = load(wnext())
                w = u.ap.rearrange("p (a b k n) -> p a b k n", a=2, b=4, k=2)
                for hf in range(2):
                    tr, ti = {}, {}
                    for cc in range(4):
                        c = 4 * hf + cc
                        blk, m = c // 2, c % 2
                        for a, (dst, bn, td) in enumerate(((R_, "br", tr), (I_, "bi", ti))):
                            b = bank()
                            t = mm_group(banks[b][:], [(w[:, a, blk, k, m * P:(m + 1) * P], uc[:, 2 * blk + k, :]) for k in range(2)], True,
                                         u.tok, *bank_free[b], uct[2 * blk], uct[2 * blk + 1])
                            t = C.act(lambda e, b=b, dst=dst, cc=cc, c=c, bn=bn, d=d: e.activation(
                                dst[:, cc, :], banks[b][:], ACT.Sigmoid, bias=cs(bn)[:, 8 * d + c:8 * d + c + 1]), t, *fr)
                            bank_free[b] = [t]
                            td[cc] = t
                    tM, tI_ = {}, {}
                    for cc in range(4):
                        c = 4 * hf + cc
                        sp_ = nspt[:, 8 * d + c:8 * d + c + 1]
                        tT = C.act(lambda e, cc=cc, sp_=sp_: e.activation(T_[:, cc, :], R_[:, cc, :], ACT.Tanh, scale=sp_), tr[cc], t_nsp, *fr)
                        tA = C.act(lambda e, cc=cc, sp_=sp_: e.activation(R_[:, cc, :], R_[:, cc, :], ACT.Exp, scale=sp_), tT)
                        tI = C.dve(lambda e, cc=cc, c=c: e.tensor_tensor(I_[:, cc, :], I_[:, cc, :], uc[:, c, :], ALU.mult), ti[cc])
                        x1 = up[:, cc % 2, 0:512]
                        t = C.dve(lambda e, cc=cc, x1=x1: e.tensor_tensor(x1, R_[:, cc, :], R_[:, cc, :], ALU.mult), tA, *fr)
                        tM[cc] = C.dve(lambda e, cc=cc, x1=x1: e.scalar_tensor_tensor(T_[:, cc, :], x1, 1.0, T_[:, cc, :], ALU.add, ALU.mult), t)
                        tI_[cc] = tI
                    for cc in range(4):
                        c = 4 * hf + cc
                        t = C.act(lambda e, cc=cc: e.activation(T_[:, cc, :], T_[:, cc, :], ACT.Sqrt, scale=-1.0, bias=tiny[:, 0:1]), tM[cc])
                        t = C.dve(lambda e, cc=cc: e.tensor_tensor(I_[:, cc, :], I_[:, cc, :], T_[:, cc, :], ALU.mult), t, tI_[cc])
                        if d == 0:
                            t = C.dve(lambda e, cc=cc, c=c: e.tensor_tensor_scan(hs[:, c, :], R_[:, cc, :], I_[:, cc, :], 0.0, ALU.mult, ALU.add), t)
                            hst[c] = t
                        else:
                            t = C.dve(lambda e, cc=cc: e.tensor_tensor_scan(T_[:, cc, ::-1], R_[:, cc, ::-1], I_[:, cc, ::-1], 0.0, ALU.mult, ALU.add), t)
                            t = C.dve(lambda e, cc=cc, c=c: e.tensor_tensor(hs[:, c, :], hs[:, c, :], T_[:, cc, :], ALU.add), t, hst[c])
                            t = C.dve(lambda e, c=c: e.tensor_tensor(yT[:, c, :], yT[:, c, :], hs[:, c, :], ALU.mult), t, yt[c])
                        last = t
                    fr = [last]
                release(u, C.last("pe"))
            out_proj(yT, [last], [wnext(), wnext()])

        def attention():
            entry = [C.last("pe"), C.last("dve"), C.last("act")]
            stage = ar(4096, 2048).rearrange("p (b d) -> p b d", b=2)
            junk = ar(6144, 1024)
            outs = norm_rows(6, lambda i: h[:, i, :], lambda i: [], junk)
            for i in range(NT):
                h_tok[i] = [outs[i]]
            xT = ar(0, 4096).rearrange("p (k s) -> p k s", k=KT)
            QK = ar(4096, 8704).rearrange("p (j s) -> p j s", j=17)
            V = ar(12800, 1536).rearrange("p (t c) -> p t c", t=NT)
            A = ar(14336, 2048).rearrange("p (j s) -> p j s", j=4)
            Z = ar(16384, 4096).rearrange("p (t c) -> p t c", t=NT)
            GT = ar(20480, 112).rearrange("p (t c) -> p t c", t=NT)
            DMo = 20592
            Wk = 21744
            res = norm_T(7, xT, ar(16384, 2048), ar(18432, 1024))
            gf = gbuf[:].rearrange("p b d -> p (b d)")
            hg, hgc = gf[:, 0:HG], gf[:, HG - 128:HG]
            ksq2 = gf[:, 1536:1664]
            mx8 = gf[:, 1664:1696].rearrange("p (t c) -> p t c", t=NT)
            l_hg = Lane(nc, ctx, "l_hg")
            t_hg = l_hg.dma(C, "pool", lambda e: e.dma_start(hg, t_["hgain"].broadcast_to([P, HG])), C.last("dve"))
            entry = [C.last("pe"), C.last("dve"), C.last("act")]
            cosb = cs("cos").rearrange("p (t c) -> p t c", t=NT)
            sinb = cs("sin").rearrange("p (t c) -> p t c", t=NT)
            stg = ar(16384, 4096).rearrange("p (b c) -> p b c", b=2)
            t2b = ar(Wk, 512)
            pend = {}
            ssq = small[:, 24:56]
            qkt = {}
            cnt = [0]

            def rope_block(src, dst, nh, cos, sin, tmp, rows, *tk):
                def hv(a, half):
                    return a.rearrange("p (n c) -> p n c", c=64)[:, :, 32 * half:32 * half + 32]
                cb = cos.unsqueeze(1).broadcast_to([rows, nh, 32])
                sbb = sin.unsqueeze(1).broadcast_to([rows, nh, 32])
                s1, s2, d1, d2 = hv(src, 0), hv(src, 1), hv(dst, 0), hv(dst, 1)
                u1, u2 = hv(tmp, 0), hv(tmp, 1)
                a = C.dve(lambda e: e.tensor_tensor(d1, s1, cb, ALU.mult), *tk)
                b = C.dve(lambda e: e.tensor_tensor(u1, s2, sbb, ALU.mult), *tk)
                c = C.dve(lambda e: e.tensor_tensor(d2, s2, cb, ALU.mult), *tk)
                d = C.dve(lambda e: e.tensor_tensor(u2, s1, sbb, ALU.mult), *tk)
                C.dve(lambda e: e.tensor_tensor(d1, d1, u1, ALU.subtract), a, b)
                return C.dve(lambda e: e.tensor_tensor(d2, d2, u2, ALU.add), c, d)

            def head_norm(x, sq, gain, nh, rows, ss, *tk):
                x3 = x.rearrange("p (n c) -> p n c", c=64)
                t = C.dve(lambda e: e.tensor_tensor(sq, x, x, ALU.mult), *tk)
                t = C.dve(lambda e: e.tensor_reduce(ss, sq.rearrange("p (n c) -> p n c", c=64), X, ALU.add), t)
                t = C.dve(lambda e: e.tensor_scalar(ss, ss, 1.0 / 64, EPS, ALU.mult, ALU.add), t)
                t = C.act(lambda e: e.activation(ss, ss, ACT.Sqrt), t)
                t = C.dve(lambda e: e.reciprocal(ss, ss), t)
                t = C.dve(lambda e: e.tensor_tensor(x3, x3, ss.unsqueeze(2).broadcast_to([rows, nh, 64]), ALU.mult), t)
                return C.dve(lambda e: e.tensor_tensor(x, x, gain, ALU.mult), t)

            queue = []

            def flush(keep):
                while len(queue) > keep:
                    queue.pop(0)()

            def transposes(src, npair, toks, key, i, dest, fin):
                def go():
                    b0 = 0
                    while b0 < npair:
                        m = min(4, npair - b0)
                        b = bank()
                        for k in range(m):
                            s_ = src(b0 + k)
                            t = C.pe(lambda e, b=b, k=k, s_=s_: e.transpose(banks[b][:, k * P:(k + 1) * P], s_, ident), *toks, *bank_free[b], inc=(k == m - 1))
                        t = C.act(lambda e, b=b, m=m, b0=b0: e.activation(dest(b0, m), banks[b][:, 0:m * P].rearrange("p (k c) -> p k c", k=m), ACT.Copy), t, *entry)
                        bank_free[b] = [t]
                        b0 += m
                    fin(t)
                queue.append(go)

            specs = [
                (8, True, 0, 8, 0), (8, True, 4, 8, 512), (6, True, 8, 0, 1024), (5, False, 14, 4, None)]
            stg_free = {}
            for c, (nh, normed, pair0, dbl, goff) in enumerate(specs):
                n = nh * 64
                u = load(wnext()[:, 0:8 * n], 8 * n)
                w = u.ap.rearrange("p (k n) -> p k n", k=KT)
                for i in range(NT):
                    j = cnt[0] % 2
                    b = bank()
                    t = mm_group(banks[b][:, 0:n], [(xT[:, k, i * P:(i + 1) * P], w[:, k, :]) for k in range(KT)], True,
                                 u.tok, *bank_free[b], *res[i])
                    pr, sq, ro = stg[:, j, 0:n], stg[:, j, 512:512 + n], stg[:, j, 1024:1024 + n]
                    fr = stg_free.get(cnt[0] - 2, entry)
                    t = C.act(lambda e, b=b, pr=pr, n=n: e.activation(pr, banks[b][:, 0:n], ACT.Copy), t, *fr, *entry)
                    bank_free[b] = [t]
                    if normed:
                        t = head_norm(pr, sq, hg[:, goff:goff + n], nh, P, ssq[:, 0:nh], t, t_hg, *fr)
                    t = rope_block(pr, ro, nh, cosb[:, i, :], sinb[:, i, :], sq, P, t, *fr)
                    if dbl >= nh:
                        src = lambda k, ro=ro: ro[:, k * P:(k + 1) * P]
                        npair = nh // 2
                    else:
                        npair = (2 * nh - dbl) // 2
                        du = stg[:, j, 0:1024] if nh == 6 else stg[:, j, 512:1024]
                        if nh == 6:
                            r3 = ro.rearrange("p (n c) -> p n c", c=64)
                            d4 = stg[:, j, 0:768].rearrange("p (n r c) -> p n r c", n=6, r=2)
                            C.dve(lambda e, d4=d4, r3=r3: e.tensor_copy(d4[:, :, 0, :], r3), t)
                            t = C.dve(lambda e, d4=d4, r3=r3: e.tensor_copy(d4[:, :, 1, :], r3), t)
                            src = lambda k, j=j: stg[:, j, k * P:(k + 1) * P]
                        else:
                            t = C.dve(lambda e, j=j: e.tensor_copy(stg[:, j, 1344:1408], stg[:, j, 1280:1344]), t)
                            src = lambda k, ro=ro, j=j: stg[:, j, 1024 + k * P:1024 + (k + 1) * P]

                    def fin(t, n_=cnt[0], c=c, i=i):
                        stg_free[n_] = [C.last("pe")]
                        qkt[(c, i)] = t
                    flush(0)
                    transposes(src, npair, [t], c, i, lambda b0, m, i=i, pair0=pair0: QK[:, pair0 + b0:pair0 + b0 + m, i * P:(i + 1) * P], fin)
                    cnt[0] += 1
                release(u, C.last("pe"))
                flush(0) if c == 3 else None
                if c < 3:
                    flush(0)
            u = load(wnext()[:, 0:8 * 284], 8 * 284)
            w = u.ap.rearrange("p (k n) -> p k n", k=KT)
            at = {}
            gate_t = {}
            tz = C.dve(lambda e: e.memset(A[64:128, :, 511:512], 0.0), *entry)
            for i in range(NT):
                j = cnt[0] % 2
                b = bank()
                t0 = mm_group(banks[b][:, 0:284], [(xT[:, k, i * P:(i + 1) * P], w[:, k, :]) for k in range(KT)], True,
                              u.tok, *bank_free[b], *res[i])
                fr = stg_free.get(cnt[0] - 2, entry)
                kv = stg[:, j, 0:512].rearrange("p (n r c) -> p n r c", n=4, r=2)
                pv = banks[b][:, 0:256].rearrange("p (n c) -> p n c", c=64)
                ta = C.act(lambda e, kv=kv, pv=pv: e.activation(kv[:, :, 0, :], pv, ACT.Copy), t0, *fr)
                tb = C.act(lambda e, kv=kv, pv=pv: e.activation(kv[:, :, 1, :], pv, ACT.Copy), t0, *fr)
                t1 = C.act(lambda e, b=b, i=i: e.activation(GT[:, i, 0:24], banks[b][:, 256:280], ACT.Sigmoid), t0, *entry)
                t2 = C.act(lambda e, b=b, i=i: e.activation(GT[:, i, 24:28], banks[b][:, 280:284], ACT.Copy, scale=0.5), t0, *entry)
                gate_t[i] = [t1, t2]
                bank_free[b] = [ta, tb, t1, t2]
                b2 = bank()
                for k in range(4):
                    t = C.pe(lambda e, b2=b2, k=k, j=j: e.transpose(banks[b2][:, k * P:(k + 1) * P], stg[:, j, k * P:(k + 1) * P], ident),
                             ta, tb, *bank_free[b2], inc=(k == 3))
                stg_free[cnt[0]] = [t]
                src = banks[b2][:].rearrange("p (k c) -> p k c", k=4)
                tc = C.act(lambda e, i=i, src=src: e.activation(A[0:64, :, i * P:(i + 1) * P], src[0:64], ACT.Copy), t)
                if i == 0:
                    td = C.dve(lambda e, src=src: e.tensor_copy(A[64:128, :, 0:127], src[64:128, :, 1:128]), t, tc, *entry)
                else:
                    td = C.dve(lambda e, i=i, src=src: e.tensor_copy(A[64:128, :, i * P - 1:(i + 1) * P - 1], src[64:128]), t, tc)
                bank_free[b2] = [tc, td]
                at[i] = [tc, td]
                cnt[0] += 1
            release(u, t0)
            a_tok = [t for i in range(NT) for t in at[i]] + [tz]
            u = load(wnext()[:, 0:8 * 384], 8 * 384)
            w = u.ap.rearrange("p (k n) -> p k n", k=KT)
            vt = {}
            for i in range(NT):
                b = bank()
                t = mm_group(banks[b][:, 0:384], [(xT[:, k, i * P:(i + 1) * P], w[:, k, :]) for k in range(KT)], True,
                             u.tok, *bank_free[b], *res[i])
                vt[i] = C.act(lambda e, b=b, i=i: e.activation(V[:, i, :], banks[b][:, 0:384], ACT.Copy), t, *entry)
                bank_free[b] = [vt[i]]
            release(u, t)
            zfree = [C.last("pe"), C.last("dve"), C.last("act")]
            sm = Wk
            hid = ar(sm, 2 * 62).rearrange("p (m n) -> p m n", m=2)
            pb = ar(sm + 124, 2)
            kcp = ar(sm + 128, 128)
            ksq = ar(sm + 256, 128)
            kro = ar(sm + 384, 256)
            cmpT = ar(sm + 640, 2 * 31).rearrange("p (g n) -> p g n", g=2)
            cmpV = ar(sm + 704, 128)
            out_ = {}
            DM, dm_t = {}, {}
            all_q = list(qkt.values())
            strip = cs("strip")
            m8 = mx8

            def side():
                cents = [C.last("dve"), C.last("act"), C.last("pe")]
                for kv in range(2):
                    u = cmp_u[kv]
                    w = u.ap.rearrange("p (j n) -> p j n", j=16)
                    pe_ = cs("kpe" if kv == 0 else "vpe")
                    b1 = cs("kb1" if kv == 0 else "vb1")
                    w2 = cs("kw2" if kv == 0 else "vw2").rearrange("p (k n) -> p k n", k=2)
                    hb = []
                    for m in range(2):
                        b = bank()
                        for g in range(2):
                            for j in range(16):
                                C.pe(lambda e, b=b, m=m, g=g, j=j, kv=kv, w=w: e.matmul(
                                    banks[b][:, g * 31:g * 31 + 31], w[:, j, m * P:(m + 1) * P],
                                    A[:, 2 * kv + g, 2 * j:2 * j + 481:16], start=(j == 0), stop=(j == 15)),
                                    u.tok, *a_tok, *bank_free[b], inc=False)
                        for j in range(16):
                            t = C.pe(lambda e, b=b, m=m, j=j, w=w, pe_=pe_: e.matmul(
                                banks[b][:, 62:63], w[:, j, m * P:(m + 1) * P], pe_[:, j:j + 1], start=(j == 0), stop=(j == 15)), inc=(j == 15))
                        t1 = C.dve(lambda e, b=b, m=m, b1=b1: e.tensor_tensor(pb[:, m:m + 1], banks[b][:, 62:63], b1[:, m:m + 1], ALU.add), t, *cents)
                        t2 = C.act(lambda e, b=b, m=m: e.activation(hid[:, m, :], banks[b][:, 0:62], ACT.Silu, bias=pb[:, m:m + 1]), t1, *cents)
                        bank_free[b] = [t1, t2]
                        hb.append(t2)
                        yield
                    release(u, t)
                    yield
                    b = bank()
                    for g in range(2):
                        t = mm_group(banks[b][0:31, 64 * g:64 * g + 64], [(hid[:, m, g * 31:(g + 1) * 31], w2[:, m, :]) for m in range(2)], True,
                                     *hb, *bank_free[b])
                    cents = [t]
                    dst = kcp if kv == 0 else cmpV
                    tv = C.dve(lambda e, b=b, dst=dst: e.tensor_copy(dst[0:31, :], banks[b][0:31, 0:128]), t, hb[-1])
                    bank_free[b] = [tv]
                    if kv == 0:
                        t = head_norm(kcp[0:31, :], ksq[0:31, :], hgc[0:31, :], 2, 31, ssq[0:31, 0:2], tv, t_hg)
                        kr2 = kro[0:31, :].rearrange("p (n r c) -> p n r c", n=2, r=2)
                        t = rope_block(kcp[0:31, :], ksq2[0:31, :], 2, cs("ccos")[0:31, :], cs("csin")[0:31, :], ksq[0:31, :], 31, t)
                        k3 = ksq2[0:31, :].rearrange("p (n c) -> p n c", c=64)
                        C.dve(lambda e, kr2=kr2, k3=k3: e.tensor_copy(kr2[:, :, 0, :], k3), t)
                        t = C.dve(lambda e, kr2=kr2, k3=k3: e.tensor_copy(kr2[:, :, 1, :], k3), t)
                        yield
                        b = bank()
                        for g in range(2):
                            tp = C.pe(lambda e, b=b, g=g: e.transpose(banks[b][:, 31 * g:31 * g + 31], kro[0:31, g * P:(g + 1) * P], ident[0:31, 0:31]),
                                      t, *bank_free[b], inc=(g == 1))
                        out_['T'] = C.dve(lambda e, b=b: e.tensor_copy(ar(sm + 640, 62), banks[b][:, 0:62]), tp)
                        bank_free[b] = [out_['T']]
                    else:
                        out_['V'] = tv

                o = DMo
                for i in range(1, NT):
                    DM[i] = ar(o, (i + 1) * P)
                    o += (i + 1) * P
                assert o <= Wk
                af = [C.last("pe"), C.last("dve"), C.last("act")]
                RL = [ar(15360 + 512 * j, 512) for j in range(2)]
                rl_free = {}
                n_rl = 0
                for i in range(1, NT):
                    nk = (i + 1) * P
                    t = None
                    for hd in range(4):
                        b = bank()
                        base = 64 * (hd % 2)
                        tm = C.pe(lambda e, b=b, base=base, hd=hd, i=i, nk=nk: e.matmul(
                            banks[b][:, 0:nk], QK[base:base + 64, 14 + hd // 2, i * P:(i + 1) * P], QK[base:base + 64, 16, 0:nk], start=True, stop=True),
                            *all_q, *bank_free[b])
                        j = n_rl % 2
                        tr = C.act(lambda e, b=b, j=j, nk=nk: e.activation(RL[j][:, 0:nk], banks[b][:, 0:nk], ACT.Relu, scale=0.125), tm, *rl_free.get(n_rl - 2, []), *af)
                        bank_free[b] = [tr]
                        wi_ = GT[:, i, 24 + hd:25 + hd]
                        if hd == 0:
                            t = C.dve(lambda e, j=j, nk=nk, wi_=wi_, i=i: e.tensor_scalar(DM[i], RL[j][:, 0:nk], wi_, None, ALU.mult), tr, *gate_t[i], *af)
                        else:
                            t = C.dve(lambda e, j=j, nk=nk, wi_=wi_, i=i: e.scalar_tensor_tensor(DM[i], RL[j][:, 0:nk], wi_, DM[i], ALU.mult, ALU.add), tr, t)
                        rl_free[n_rl] = [t]
                        n_rl += 1
                        yield
                    so_ = strip[:, 384 - P * i:512]
                    t = C.dve(lambda e, i=i, so_=so_: e.tensor_tensor(DM[i], DM[i], so_, ALU.add), t)
                    dm_t[i] = t


            def dm_steps():
                for i in range(1, NT):
                    t = dm_t[i]
                    for _ in range(16):
                        t = C.dve(lambda e, i=i: e.max(m8[:, i, :], DM[i]), t)
                        t = C.dve(lambda e, i=i: e.match_replace(DM[i], m8[:, i, :], DM[i], -3e30), t)
                        yield
                    so_ = strip[:, 384 - P * i:512]
                    t = C.dve(lambda e, i=i: e.tensor_scalar(DM[i], DM[i], -2.5e30, NEG, ALU.is_gt, ALU.mult), t)
                    dm_t[i] = C.dve(lambda e, i=i, so_=so_: e.tensor_tensor(DM[i], DM[i], so_, ALU.min), t)
                    yield


            steps = dm_steps()
            sides = side()
            at_side = [True]

            def aside(n):
                for _ in range(n):
                    if at_side[0] and next(sides, StopIteration) is StopIteration:
                        at_side[0] = False
                    if not at_side[0]:
                        next(steps, None)
                        next(steps, None)

            cmp_u = [load(wnext()), load(wnext())]
            aside(2)
            zt = {}
            for c in range(2):
                u = load(wnext())
                w = u.ap.rearrange("p (k n) -> p k n", k=KT)
                for i in range(NT):
                    b = bank()
                    t = mm_group(banks[b][:], [(xT[:, k, i * P:(i + 1) * P], w[:, k, :]) for k in range(KT)], True,
                                 u.tok, *bank_free[b], *res[i])
                    zt[(c, i)] = C.act(lambda e, b=b, i=i, c=c: e.activation(Z[:, i, 512 * c:512 * c + 512], banks[b][:], ACT.Silu), t, *zfree)
                    bank_free[b] = [zt[(c, i)]]
                    aside(3)
                release(u, t)
            proj_done = C.last("pe")

            while at_side[0]:
                aside(1)
            t_cmpT, t_cmpV = out_["T"], out_["V"]
            scratch = reserve()
            DEEP = 4
            sc = [scratch.ap[:, 512 * j:512 * j + 512] for j in range(DEEP)]
            PTb = [scratch.ap[:, 512 * (DEEP + j):512 * (DEEP + j + 1)] for j in range(DEEP)]
            w_out = [load(wnext()), load(wnext())]
            MX = ar(0, 4096).rearrange("p (t c) -> p t c", t=NT)
            st = small[:, 24:56]
            state = dict(n=0)
            free_s, free_pt, mx_t, free_c = {}, {}, {}, {}

            def branch(i, qh, qpair, kp, v_ap, mask, col, coef, nkeys, mul=None, first=True, vtoks=(), cmp=False):
                n = state["n"]
                state["n"] += 1
                j = n % DEEP
                base = 64 * (qh % 2)
                b, b2, b3 = n % 3, 3 + n % 3, 6 + n % 2
                krhs = cmpT[base:base + 64, kp, :] if cmp else QK[base:base + 64, kp, 0:nkeys]
                tm = C.pe(lambda e: e.matmul(banks[b][:, 0:nkeys], QK[base:base + 64, qpair, i * P:(i + 1) * P], krhs, start=True, stop=True),
                          *all_q, *bank_free[b], *([t_cmpT] if cmp else []))
                s_ = sc[j][:, 0:nkeys]
                nm = st[:, n % 8:n % 8 + 1]
                lrow = st[:, 8 + n % 8:9 + n % 8]
                cf = st[:, 16 + n % 8:17 + n % 8]
                nb = (nkeys + P - 1) // P
                yield
                mk, mtok = mask()
                t = C.dve(lambda e: e.tensor_tensor_reduce(s_, banks[b][:, 0:nkeys], mk, -SCALE, 3e38, ALU.add, ALU.min, nm),
                          tm, *mtok, *free_s.get(n - DEEP, []), *scratch.free)
                bank_free[b] = [t]
                te = C.act(lambda e: e.activation(s_, s_, ACT.Exp, bias=nm, scale=-1.0, accum_out=lrow), t)
                yield
                yield
                t = te
                if mul is not None:
                    t = C.dve(lambda e: e.tensor_tensor(s_, s_, mul, ALU.mult), te)
                for k in range(nb):
                    w_ = min(P, nkeys - k * P)
                    tp = C.pe(lambda e, k=k, w_=w_: e.transpose(banks[b2][0:w_, k * P:(k + 1) * P], s_[:, k * P:k * P + w_], ident),
                              t, *bank_free[b2], inc=(k == nb - 1))
                free_s[n] = [tp]
                t2 = C.dve(lambda e: e.reciprocal(cf, lrow), te)
                if coef is not None:
                    t2 = C.dve(lambda e: e.tensor_tensor(cf, cf, coef, ALU.mult), t2, *gate_t[i])
                yield
                rows = min(P, nkeys)
                te2 = C.act(lambda e: e.activation(PTb[j][0:rows, 0:nb * P], banks[b2][0:rows, 0:nb * P], ACT.Copy), tp, *free_pt.get(n - DEEP, []), *scratch.free)
                bank_free[b2] = [te2]
                yield
                for k in range(nb):
                    w_ = min(P, nkeys - k * P)
                    tq = C.pe(lambda e, k=k, w_=w_: e.matmul(banks[b3][:, 0:64], PTb[j][0:w_, k * P:(k + 1) * P], v_ap(k), start=(k == 0), stop=(k == nb - 1)),
                              te2, *vtoks, *bank_free[b3], inc=(k == nb - 1))
                free_pt[n] = [tq]
                yield
                dst = MX[:, i, col:col + 64]
                if first:
                    to = C.dve(lambda e: e.tensor_scalar(dst, banks[b3][:, 0:64], cf, None, ALU.mult), tq, t2, proj_done)
                else:
                    to = C.dve(lambda e: e.scalar_tensor_tensor(dst, banks[b3][:, 0:64], cf, dst, ALU.mult, ALU.add), tq, t2, mx_t[(i, col)])
                bank_free[b3] = [to]
                mx_t[(i, col)] = to
                free_c[n] = [to]

            vts = [vt[i] for i in range(NT)]
            cadd = cs("cmpadd").rearrange("p (t n) -> p t n", t=NT)
            cmul = cs("cmpmul").rearrange("p (t n) -> p t n", t=NT)
            work = []
            for i in range(NT):
                nk = (i + 1) * P
                caus = (strip[:, 384 - P * i:512], [])
                for hd in range(8):
                    g = hd // 4
                    gc = lambda r, hd=hd, i=i: GT[:, i, 3 * hd + r:3 * hd + r + 1]
                    work.append(lambda i=i, hd=hd, g=g, gc=gc: branch(i, hd, hd // 2, g, lambda k, g=g: cmpV[0:31, 64 * g:64 * g + 64],
                                lambda i=i: (cadd[:, i, :], []), 64 * hd, gc(0), 31, mul=cmul[:, i, :], first=True, vtoks=[t_cmpV], cmp=True))
                    work.append(lambda i=i, hd=hd, g=g, gc=gc, nk=nk, caus=caus: branch(i, hd, hd // 2, 8 + g, lambda k, g=g: V[:, k, 64 * g:64 * g + 64],
                                lambda caus=caus: caus, 64 * hd, gc(1), nk, first=False, vtoks=vts))
                    work.append(lambda i=i, hd=hd, g=g, gc=gc, nk=nk, caus=caus: branch(i, hd, hd // 2, 10 + g, lambda k, g=g: V[:, k, 128 + 64 * g:192 + 64 * g],
                                lambda caus=caus: caus, 64 * hd, gc(2), nk, first=False, vtoks=vts))
            n_nsa = len(work)
            for i in range(NT):
                nk = (i + 1) * P
                caus = (strip[:, 384 - P * i:512], [])
                for hd in range(8):
                    g = hd // 4
                    mk = lambda i=i, caus=caus: caus if i == 0 else (DM[i], [dm_t[i]])
                    work.append(lambda i=i, hd=hd, g=g, nk=nk, mk=mk: branch(i, hd, 4 + hd // 2, 12 + g, lambda k, g=g: V[:, k, 256 + 64 * g:320 + 64 * g],
                                mk, 512 + 64 * hd, None, nk, first=True, vtoks=vts))
            live = []
            for n_ in range(len(work) + 8):
                if n_ == n_nsa:
                    for _ in steps:
                        pass
                live = [x for x in live if next(x, StopIteration) is not StopIteration]
                if n_ < len(work):
                    x = work[n_]()
                    next(x)
                    live.append(x)
                if n_ % 2:
                    next(steps, None)
            assert not live

            mT = QK_as = ar(4096, 4096).rearrange("p (k s) -> p k s", k=KT)
            done_qk = [C.last("pe"), C.last("act")]
            mt = []
            for i in range(NT):
                t = C.dve(lambda e, i=i: e.tensor_tensor(MX[:, i, :], MX[:, i, :], Z[:, i, :], ALU.mult), C.last("dve"), zt[(0, i)], zt[(1, i)])
                C.wait("dve", *done_qk)
                d_, _ = transposed(mT, MX[:, i, :], [t], i)
                mt += d_
            us = w_out
            l_o = Lane(nc, ctx, "l_o")
            for i in range(NT):
                for c in range(2):
                    u = us[c]
                    w = u.ap.rearrange("p (k n) -> p k n", k=KT)
                    b = bank()
                    t = mm_group(banks[b][:], [(mT[:, k, i * P:(i + 1) * P], w[:, k, :]) for k in range(KT)], True,
                                 u.tok, *bank_free[b], *mt)
                    t = add_to_h(i, 512 * c, 512, b, t)
                to = l_o.dma(C, "pool", lambda e, i=i: e.dma_start(t_["out"][i * P:(i + 1) * P, :], h[:, i, :]), t)
            for e in C.q:
                C.wait(e, to)

        mixer_a()
        moe(0)
        ple(0)
        mixer_b()
        moe(1)
        ple(1)
        attention()
        assert wat[0] == W.shape[0], (wat[0], W.shape)

        block = ctx.enter_context(nc.Block())
        for deco, name in ((block.sync, "sp"), (block.tensor, "pe"), (block.vector, "dve"), (block.scalar, "act"), (block.gpsimd, "pool")):
            @deco
            def _(e, name=name):
                for f in C.q[name]:
                    f(e)


def _units(w, widths=None):
    K, N = w.shape
    out, a = [], 0
    for n in (widths or [512] * (N // 512)):
        u = w[:, a:a + n].reshape(K // P, P, n).transpose(1, 0, 2).reshape(P, -1)
        if u.shape[1] < UNIT:
            u = np.concatenate([u, np.zeros((P, UNIT - u.shape[1]), u.dtype)], axis=1)
        out.append(u)
        a += n
    return out


def _cols(v, n):
    return np.moveaxis(v.reshape(*v.shape[:-1], n, P), -1, 0).reshape(P, -1)


def _shape_tables():
    f = np.float32
    tb = {}
    tb["ident"] = np.eye(P, dtype=f)
    tb["tri"] = np.triu(np.ones((P, P), f), 1)
    p = np.arange(P)[:, None]
    tb["strip"] = np.where(np.arange(512)[None, :] <= p + 384, 0.0, NEG).astype(f)
    tb["ones"] = np.ones((P, 128), f)
    t = np.arange(S).reshape(NT, P).T[:, :, None]
    end = (np.arange(NCMP) * 16 + 31)[None, None, :]
    tb["cmpmul"] = (end <= t).astype(f).reshape(P, -1)
    tb["cmpadd"] = np.where(end <= t, 0.0, NEG).astype(f).reshape(P, -1)
    inv = (f(10000.0) ** (-np.arange(32, dtype=f) / f(32))).astype(f)
    ang = (t.astype(f) * inv[None, None, :]).astype(f)
    tb["cos"], tb["sin"] = np.cos(ang).reshape(P, -1), np.sin(ang).reshape(P, -1)
    ca = np.zeros((P, 32), f)
    ca[:NCMP] = (np.arange(NCMP) * 16 + 31).astype(f)[:, None] * inv[None, :]
    tb["ccos"], tb["csin"] = np.cos(ca), np.sin(ca)
    tb["rev4"] = np.tile(np.arange(4, 0, -1).astype(f), (P, 1))
    tb["rev8"] = np.tile(np.arange(8, 0, -1).astype(f), (P, 1))
    tb["iota32"] = np.tile(np.arange(NE).astype(f), (P, 1))
    tb["iotab"] = np.tile(np.arange(NOVF).astype(f), (P, 1))
    tb["tok"] = np.arange(S).reshape(NT, P).T.astype(f)
    return tb


def kernel(**inputs):
    import concourse.bacc as _bacc
    from concourse.bass_utils import run_bass_kernel_spmd as _run

    v = {k: np.asarray(a) for k, a in inputs.items()}
    tb = _shape_tables()
    tb["conva"] = _cols(v["conv_a"][0], 8).reshape(P, 3, 8).transpose(0, 2, 1).reshape(P, -1)
    tb["convb"] = _cols(v["conv_b"][0], 8).reshape(P, 4, 8).transpose(0, 2, 1).reshape(P, -1)
    tb["cbias"] = _cols(v["conv_bias_b"][0], 8)
    tb["br"], tb["bi"], tb["lam"] = (_cols(v[k][0], 8) for k in ("b_rgate_b", "b_igate_b", "lam_b"))
    for kv in "kv":
        tb[f"{kv}b1"] = _cols(v[f"cmp_{kv}_b1_2"][0], 2)
        tb[f"{kv}pe"] = v[f"cmp_pe_{kv}_2"][0].reshape(16, P).T
        tb[f"{kv}w2"] = v[f"cmp_{kv}_w2_2"][0].reshape(2, P, 64).transpose(1, 0, 2).reshape(P, -1)
    rb = []
    for l in range(2):
        rw = np.concatenate([v["w_router_group"][l], v["w_router_expert"][l]], axis=1)
        tb[f"rw{l}"] = rw.reshape(KT, P, 36).transpose(1, 0, 2).reshape(P, -1)
        rb += [v["b_router_group"][l], v["b_router_expert"][l]]
    tb["rb"] = np.broadcast_to(np.concatenate(rb), (P, 72))
    cst = np.concatenate([tb[n].reshape(P, w) for n, w in CST], axis=1)
    rows = np.stack([v["norm_mix"][0], v["norm_ffn"][0], v["norm_ple"][0], v["norm_mix"][1], v["norm_ffn"][1],
                     v["norm_ple"][1], v["norm_final"], v["norm_gain_2"][0]])
    q, ks, kw, kc, qd, kd = (v[k][0] for k in ("nsa_q_gain_2", "nsa_ks_gain_2", "nsa_kw_gain_2", "nsa_kc_gain_2", "dsa_q_gain_2", "dsa_k_gain_2"))
    hgain = np.concatenate([q] * 8 + [qd] * 8 + [ks] * 2 + [kw] * 2 + [kd] * 2 + [kc] * 2)[None, :]

    wall = []
    wa = _units(v["w_in_a"][0])
    for c in range(2):
        wall += [wa[c], wa[2 + c], wa[4 + c]]
    wall += _units(v["w_out_a"][0])

    def ple_units(l):
        return _units(v["w_ple"][l], [1024]) + _units(v["w_ple_gate"][l])

    wall += ple_units(0)
    wb = _units(v["w_in_b"][0])
    wall += wb[2:] + wb[:2]
    gates = np.stack([v["w_rgate_b"][0], v["w_igate_b"][0]], axis=1)
    for d in range(2):
        wall.append(gates[d].reshape(2, 4, 2, P, 256).transpose(3, 0, 1, 2, 4).reshape(P, -1))
    wall += _units(v["w_out_b"][0])
    wall += ple_units(1)
    w2 = v["w_in_2"][0]
    at, a = {}, 0
    for name, n in (("q_n", 512), ("kc", 128), ("vc", 128), ("ks", 128), ("vs", 128), ("kw", 128), ("vw", 128), ("gate", 24),
                    ("z_n", 512), ("q_d", 512), ("k_d", 128), ("v_d", 128), ("qi", 256), ("ki", 64), ("wi", 4), ("z_d", 512)):
        at[name] = w2[:, a:a + n]
        a += n
    for names in (["q_n"], ["q_d"], ["ks", "kw", "k_d"], ["qi", "ki"], ["kc", "vc", "gate", "wi"], ["vs", "vw", "v_d"], "kv", ["z_n"], ["z_d"]):
        if names == "kv":
            for kv in "kv":
                wall.append(v[f"cmp_{kv}_w1_2"][0].reshape(16, P, 256).transpose(1, 0, 2).reshape(P, -1))
            continue
        m = np.concatenate([at[x] for x in names], axis=1)
        wall += _units(m, [m.shape[1]])
    wall += _units(v["w_out_2"][0])
    wall = np.stack(wall)

    wexp = np.empty((2, NE, 3, P, UNIT), np.float32)
    wexp[:, :, 0] = v["w_exp_gate"].reshape(2, NE, KT, P, 512).transpose(0, 1, 3, 2, 4).reshape(2, NE, P, UNIT)
    wexp[:, :, 1] = v["w_exp_up"].reshape(2, NE, KT, P, 512).transpose(0, 1, 3, 2, 4).reshape(2, NE, P, UNIT)
    wexp[:, :, 2] = v["w_exp_down"].reshape(2, NE, 4, P, D).transpose(0, 1, 3, 2, 4).reshape(2, NE, P, UNIT)

    arrays = {
        "x": v["x"][0], "cst": cst, "rows": rows, "hgain": hgain, "wall": wall, "wexp": wexp,
        "pT": v["p"][:, 0].transpose(0, 2, 1).reshape(2, 2, P, S).transpose(0, 2, 1, 3).reshape(2, P, 2 * S),
        "plebias": v["b_ple_gate"],
    }
    arrays = {k: np.ascontiguousarray(a) for k, a in arrays.items()}
    nc = _bacc.Bacc("TRN2", target_bir_lowering=False, num_devices=1)
    t_ = {k: nc.dram_tensor(f"in_{k}", a.shape, mybir.dt.from_np(a.dtype), kind="ExternalInput").ap() for k, a in arrays.items()}
    t_["out"] = nc.dram_tensor("out_0", (S, D), F32, kind="ExternalOutput").ap()
    build(nc, t_)
    r = _run(nc, [{f"in_{k}": a for k, a in arrays.items()}], core_ids=[0])
    return r.results[0]["out_0"].reshape(1, S, D)
```

```python
from contextlib import ExitStack

import numpy as np

import concourse.bass as bass
from concourse import mybir

ALU = mybir.AluOpType
ACT = mybir.ActivationFunctionType
F32 = mybir.dt.float32
I32 = mybir.dt.int32
X = mybir.AxisListType.X

P = 128
S = 512
D = 1024
NT = S // P
KT = D // P
NE = 32
CAP = 64
NOVF = (2 * S) // (CAP + 1)
NB = NE + NOVF
RING = 5
UNIT = 4096
EPS = 1e-6
NEG = -1e30
SCALE = 0.125
NCMP = 31

CST = [
    ("ident", 128), ("tri", 128), ("strip", 512), ("ones", 128), ("cmpadd", 4 * NCMP), ("cmpmul", 4 * NCMP),
    ("cos", 4 * 32), ("sin", 4 * 32), ("ccos", 32), ("csin", 32),
    ("rev4", 4), ("rev8", 8), ("iota32", NE), ("iotab", NOVF), ("tok", NT), ("iotas", CAP),
    ("conva", 24), ("convb", 32), ("cbias", 8), ("br", 16), ("bi", 16), ("lam", 16),
    ("kb1", 2), ("vb1", 2), ("kpe", 16), ("vpe", 16), ("kw2", 128), ("vw2", 128),
    ("rw0", 8 * 36), ("rw1", 8 * 36), ("rb", 2 * 36),
]
OFF = {}
_o = 0
for _n, _w in CST:
    OFF[_n] = (_o, _o + _w)
    _o += _w
NCST = _o

ROWS = ["mix0", "ffn0", "ple0", "mix1", "ffn1", "ple1", "final", "att"]
HG = 22 * 64 + 128


class Core:

    def __init__(self, nc, ctx, tag, engines=("pe", "act", "dve", "pool", "sp")):
        self.sem = {e: ctx.enter_context(nc.semaphore(f"{tag}_{e}")) for e in engines}
        self.n = {e: 0 for e in engines}
        self.q = {e: [] for e in engines}
        self.seen = {e: {} for e in engines}

    def wait(self, eng, *toks):
        need = {}
        for sem, v in toks:
            if self.seen[eng].get(id(sem), 0) < v:
                need[id(sem)] = (sem, max(v, need.get(id(sem), (sem, 0))[1]))
        for k, (sem, v) in need.items():
            self.seen[eng][k] = v
            self.q[eng].append(lambda e, sem=sem, v=v: e.wait_ge(sem, v))

    def put(self, eng, fn, *toks, inc=True):
        self.wait(eng, *toks)
        if not inc:
            self.q[eng].append(fn)
            return None
        self.n[eng] += 1
        sem = self.sem[eng]
        self.q[eng].append(lambda e: fn(e).then_inc(sem, 1))
        return (sem, self.n[eng])

    def last(self, eng):
        return (self.sem[eng], self.n[eng])

    def pe(self, fn, *t, inc=True):
        return self.put("pe", fn, *t, inc=inc)

    def act(self, fn, *t):
        return self.put("act", fn, *t)

    def dve(self, fn, *t):
        return self.put("dve", fn, *t)

    def pool(self, fn, *t):
        return self.put("pool", fn, *t)


class Lane:

    def __init__(self, nc, ctx, name):
        self.sem = ctx.enter_context(nc.semaphore(name))
        self.n = 0

    def dma(self, core, eng, fn, *toks):
        core.wait(eng, *toks)
        self.n += 16
        core.q[eng].append(lambda e, s=self.sem: fn(e).then_inc(s, 16))
        return (self.sem, self.n)


def build(nc, t_):
    ctx = ExitStack()
    with ctx:
        def sb(name, shape, dt=F32):
            return ctx.enter_context(nc.sbuf_tensor(name, shape, dt))

        def dram(name, shape, dt=F32):
            return nc.dram_tensor(name, shape, dt, kind="Internal").ap()

        C = Core(nc, ctx, "m")
        ring = sb("ring", [P, RING * UNIT])
        h = sb("h", [P, NT, D])
        cst = sb("cst", [P, NCST])
        gbuf = sb("gbuf", [P, 2, D])
        small = sb("small", [P, 64])
        nspt = sb("nspt", [P, 16])
        rsb = sb("rsb", [P, 8])
        AR = 23600
        arena = sb("arena", [P, AR])
        banks = [ctx.enter_context(nc.psum_tensor(f"ps{i}", [P, 512], F32)) for i in range(8)]
        bank_free = [[] for _ in range(8)]
        bank_at = [0]

        xs_d = [dram(f"xs_d{l}", [S, D]) for l in range(2)]
        y_d = [dram(f"y_d{l}", [CAP * NB, D]) for l in range(2)]

        def cs(name):
            a, b = OFF[name]
            return cst[:, a:b]

        def ar(off, n):
            assert off + n <= AR, (off, n)
            return arena[:, off:off + n]

        def bank():
            b = bank_at[0]
            bank_at[0] = (b + 1) % 8
            return b

        ring_lane = [Lane(nc, ctx, f"ring{i}") for i in range(RING)]
        ring_free = {}
        ring_n = [0]

        class Unit:
            pass

        def load(src, width=UNIT):
            u = Unit()
            i = ring_n[0]
            ring_n[0] += 1
            u.i, s = i, i % RING
            u.ap = ring[:, s * UNIT:s * UNIT + width]
            u.tok = ring_lane[s].dma(C, "sp", lambda e, u=u: e.dma_start(u.ap, src), *(ring_free[i - RING] if i >= RING else []))
            return u

        def reserve():
            u = Unit()
            i = ring_n[0]
            ring_n[0] += 1
            u.i, s = i, i % RING
            u.ap = ring[:, s * UNIT:(s + 1) * UNIT]
            u.free = ring_free[i - RING]
            return u

        def release(u, *toks):
            ring_free[u.i] = list(toks)

        l_cst = Lane(nc, ctx, "l_cst")
        l_h = [Lane(nc, ctx, f"l_h{i}") for i in range(NT)]
        l_g = [Lane(nc, ctx, f"l_g{i}") for i in range(4)]
        g_tok = {}
        g_free = {}

        def load_gain(n):
            if n < len(ROWS):
                row = t_["rows"][n:n + 1, :].broadcast_to([P, D])
                g_tok[n] = l_g[n if n < 2 else 2 + n % 2].dma(C, "sp" if n < 2 else "pool", lambda e, n=n, row=row: e.dma_start(gbuf[:, n % 2, :], row),
                                          *(g_free[n - 2] if n >= 2 else []))

        h_tok = []
        for i in range(NT):
            h_tok.append([l_h[i].dma(C, "sp", lambda e, i=i: e.dma_start(h[:, i, :], t_["x"][i * P:(i + 1) * P, :]))])
            if i == 0:
                load_gain(0)
                t_cst = l_cst.dma(C, "sp", lambda e: e.dma_start(cst[:], t_["cst"]))
        load_gain(1)

        ident = cs("ident")
        ones = cs("ones")

        def softplus_neg8():
            w = ar(21000, 128)
            x_, a_, y_, z_, q_, s_ = (w[:, 16 * i:16 * i + 16] for i in range(6))
            lam = cs("lam")
            t = C.dve(lambda e: e.tensor_scalar(x_, lam, -1.0, None, ALU.mult), t_cst)
            t = C.dve(lambda e: e.tensor_tensor(a_, x_, lam, ALU.min), t)
            t = C.act(lambda e: e.activation(y_, a_, ACT.Exp), t)
            t = C.dve(lambda e: e.tensor_scalar(z_, y_, 2.0, None, ALU.add), t)
            t = C.dve(lambda e: e.reciprocal(z_, z_), t)
            t = C.dve(lambda e: e.tensor_tensor(z_, z_, y_, ALU.mult), t)
            t = C.dve(lambda e: e.tensor_tensor(q_, z_, z_, ALU.mult), t)
            t = C.dve(lambda e: e.tensor_scalar(s_, q_, 1.0 / 19, 1.0 / 17, ALU.mult, ALU.add), t)
            for n in (15, 13, 11, 9, 7, 5, 3, 1):
                t = C.dve(lambda e: e.tensor_tensor(s_, s_, q_, ALU.mult), t)
                t = C.dve(lambda e, n=n: e.tensor_scalar(s_, s_, 1.0 / n, None, ALU.add), t)
            t = C.dve(lambda e: e.tensor_tensor(s_, s_, z_, ALU.mult), t)
            t = C.dve(lambda e: e.tensor_scalar(x_, x_, 0.0, None, ALU.max), t)
            t = C.dve(lambda e: e.scalar_tensor_tensor(x_, s_, 2.0, x_, ALU.mult, ALU.add), t)
            return C.dve(lambda e: e.tensor_scalar(nspt[:], x_, -8.0, None, ALU.mult), t)

        tiny = small[:, 56:57]
        t_tiny = C.dve(lambda e: e.memset(tiny, 1e-30))
        arena_free = [t_tiny]

        evac_at = [0]

        def evac(out, in_, *toks):
            evac_at[0] += 1
            if evac_at[0] % 2:
                return C.act(lambda e: e.activation(out, in_, ACT.Copy), *toks)
            return C.dve(lambda e: e.tensor_copy(out, in_), *toks)

        def transposed(xT, src, toks, i):
            done = []
            for hf in range(2):
                b = bank()
                for k in range(4):
                    kk = 4 * hf + k
                    t = C.pe(lambda e, b=b, k=k, kk=kk: e.transpose(banks[b][:, k * P:(k + 1) * P], src[:, kk * P:(kk + 1) * P], ident),
                             *(bank_free[b] if k == 0 else []), *toks, t_cst, inc=(k == 3))
                t = evac(xT[:, 4 * hf:4 * hf + 4, i * P:(i + 1) * P], banks[b][:].rearrange("p (k c) -> p k c", k=4), t)
                bank_free[b] = [t]
                done.append(t)
            return done, C.last("pe")

        class Norm:

            def __init__(self, n, stage, junk, also=None, first=None, toks=()):
                self.n, self.junk, self.also, self.first = n, junk, also, first
                self.nb = stage.shape[1] // D if stage is not None else 0
                self.xs = stage.rearrange("p (b d) -> p b d", b=self.nb) if stage is not None else None
                self.xT = ar(0, 4096).rearrange("p (k s) -> p k s", k=KT)
                self.safe = list(toks)
                self.used, self.row_t, self.res = {}, {}, {}

            def rows(self, i):
                if self.first:
                    self.first.rows(i)
                n = self.n
                k = 4 * (n % 2) + i
                rs = rsb[:, k:k + 1]
                dst = self.xs[:, i % self.nb, :] if self.xs is not None else h[:, i, :]
                t = C.act(lambda e: e.activation(self.junk, h[:, i, :], ACT.Square, accum_out=rs), *h_tok[i], *self.safe)
                t = C.dve(lambda e: e.tensor_scalar(rs, rs, 1.0 / D, EPS, ALU.mult, ALU.add), t)
                t = C.act(lambda e: e.activation(rs, rs, ACT.Sqrt), t)
                t = C.dve(lambda e: e.reciprocal(rs, rs), t)
                t = C.dve(lambda e: e.scalar_tensor_tensor(dst, h[:, i, :], rs, gbuf[:, n % 2, :], ALU.mult, ALU.mult),
                          t, g_tok[n], *self.used.get(i - self.nb, []), *self.safe)
                if self.xs is None:
                    h_tok[i] = [t]
                self.row_t[i] = t
                self.extra = self.also(i, dst, t) if self.also else []
                self.used[i] = list(self.extra)
                if i == NT - 1:
                    g_free[n] = [t]
                    load_gain(n + 2)

            def trans(self, i):
                done, last = transposed(self.xT, self.xs[:, i % self.nb, :], [self.row_t[i]], i)
                self.used[i].append(last)
                self.res[i] = done

            def feed(self, i):
                self.rows(i)

            def behind(self, i):
                if i >= 1:
                    self.trans(i - 1)

            def finish(self):
                self.trans(NT - 1)

        def mm_group(out_b, pairs, first, *toks, bias=None, width=512, rows=P):
            n = len(pairs)
            for j, (l, r) in enumerate(pairs):
                t = C.pe(lambda e, l=l, r=r, j=j: e.matmul(out_b, l, r, start=(j == 0), stop=(j == n - 1)),
                         *(toks if j == 0 else []), inc=(j == n - 1))
            return t

        def add_to_h(i, lo, n, b, t):
            t = C.dve(lambda e: e.tensor_tensor(h[:, i, lo:lo + n], h[:, i, lo:lo + n], banks[b][:, 0:n], ALU.add), t, *h_tok[i])
            bank_free[b] = [t]
            return t

        def out_proj(gT, g_toks, units, nxt):
            nxt.safe += [C.last("pe"), C.last("act"), C.last("dve")]
            for c, src in enumerate(units):
                u = load(src)
                w = u.ap.rearrange("p (k n) -> p k n", k=KT)
                for i in range(NT):
                    b = bank()
                    t = mm_group(banks[b][:], [(gT[:, k, i * P:(i + 1) * P], w[:, k, :]) for k in range(KT)], True,
                                 u.tok, *bank_free[b], *g_toks)
                    if i == NT - 1:
                        release(u, t)
                    h_tok[i] = [add_to_h(i, 512 * c, 512, b, t)]
                    if c == 1:
                        nxt.feed(i)
                        nxt.behind(i)
            nxt.finish()

        W = t_["wall"]
        wat = [0]

        def wnext():
            wat[0] += 1
            return W[wat[0] - 1]

        l_cy = [Lane(nc, ctx, f"l_cy{l}") for l in range(2)]
        cy_t = []

        def clear_y():
            z = ar(AR - D, D)
            t = C.dve(lambda e: e.memset(z, 0.0))
            for l in range(2):
                cy_t.append(l_cy[l].dma(C, "sp", lambda e, l=l: e.dma_start(
                    y_d[l].rearrange("(s b) d -> s b d", b=NB)[:, NE:, :], z[0:CAP, :].unsqueeze(1).broadcast_to([CAP, NOVF, D])), t))

        nsp_tok = []

        def mixer_a(N, nxt):
            xT = N.xT
            gT = ar(4096, 4096).rearrange("p (k s) -> p k s", k=KT)
            for i in range(NT):
                N.feed(i)
                N.behind(i)
            N.finish()
            nsp_tok.append(softplus_neg8())
            xt = [t for r in N.res.values() for t in r]
            cS = ar(11264, 1024).rearrange("p (b s) -> p b s", b=2)
            v = ar(12288, 1028).rearrange("p (b s) -> p b s", b=2)
            u1 = ar(13316, 1024).rearrange("p (b s) -> p b s", b=2)
            tz = C.dve(lambda e: e.memset(v, 0.0), *arena_free)
            ca = cs("conva").rearrange("p (c k) -> p c k", c=8)
            freec, gt = {}, []
            for q in range(2):
                us = [load(wnext()) for _ in range(3)]
                if q == 1:
                    clear_y()
                for c4 in range(4):
                    c = 4 * q + c4
                    bs, ts = [], []
                    for u in us:
                        b = bank()
                        w = u.ap.rearrange("p (k n) -> p k n", k=KT)
                        ts.append(mm_group(banks[b][:], [(w[:, k, c4 * P:(c4 + 1) * P], xT[:, k, :]) for k in range(KT)], True,
                                           u.tok, *bank_free[b], *xt))
                        bs.append(b)
                        if c4 == 3:
                            release(u, ts[-1])
                    j = c % 2
                    t1 = C.act(lambda e, j=j, b=bs[1]: e.activation(cS[:, j, :], banks[b][:], ACT.Copy), ts[1], *freec.get(c - 2, []))
                    bank_free[bs[1]] = [t1]
                    t = C.dve(lambda e, j=j, b=bs[2]: e.tensor_tensor(v[:, j, 1:513], cS[:, j, :], banks[b][:], ALU.mult),
                              t1, ts[2], tz, *freec.get(c - 2, []))
                    bank_free[bs[2]] = [t]
                    t = C.act(lambda e, j=j, c=c: e.activation(u1[:, j, :], v[:, j, 0:512], ACT.Copy, scale=ca[:, c, 0:1]), t, *freec.get(c - 2, []))
                    t = C.dve(lambda e, j=j, c=c: e.scalar_tensor_tensor(u1[:, j, :], v[:, j, 1:513], ca[:, c, 1:2], u1[:, j, :], ALU.mult, ALU.add), t)
                    t = C.dve(lambda e, j=j, c=c: e.scalar_tensor_tensor(u1[:, j, :], v[:, j, 2:514], ca[:, c, 2:3], u1[:, j, :], ALU.mult, ALU.add), t)
                    t = C.dve(lambda e, j=j, c=c, b=bs[0]: e.tensor_tensor(gT[:, c, :], u1[:, j, :], banks[b][:], ALU.mult), t, ts[0])
                    bank_free[bs[0]] = [t]
                    freec[c] = [t]
                    gt = [t]
            out_proj(gT, gt, [wnext(), wnext()], nxt)

        def moe(l, N, nxt, xs_t):
            xT, res = N.xT, N.res
            lg = ar(11264, 144).rearrange("p (t e) -> p t e", t=NT)
            rw = cs(f"rw{l}").rearrange("p (k e) -> p k e", k=KT)
            rb = cs("rb")[0:1, l * 36:(l + 1) * 36]
            b = bank()
            for i in range(NT):
                o = banks[b][:, i * 36:(i + 1) * 36]
                t = C.pe(lambda e, o=o: e.matmul(o, ones[0:1, :], rb, start=True, stop=False), *bank_free[b], *res[i], inc=False)
                for k in range(KT):
                    t = C.pe(lambda e, k=k, o=o, i=i: e.matmul(o, xT[:, k, i * P:(i + 1) * P], rw[:, k, :], start=False, stop=(k == 7)), inc=(k == 7))
            t = C.dve(lambda e, b=b: e.tensor_copy(ar(11264, 144), banks[b][:, 0:144]), t)
            bank_free[b] = [t]
            G = lg[:, :, 0:4]
            L = lg[:, :, 4:36].rearrange("p t (g e) -> p t g e", g=4)
            so = [11520]

            def alloc(*dims):
                w = int(np.prod(dims))
                a = ar(so[0], w)
                so[0] += w
                if len(dims) == 2:
                    a = a.rearrange("p (a b) -> p a b", a=dims[0])
                if len(dims) == 3:
                    a = a.rearrange("p (a b c) -> p a b c", a=dims[0], b=dims[1])
                return a

            def TT(out, a, b_, op, *tk):
                return C.dve(lambda e: e.tensor_tensor(out, a, b_, op), *tk)

            def RD(out, a, op, *tk):
                return C.dve(lambda e: e.tensor_reduce(out, a, X, op), *tk)

            def TS(out, a, s1, op, *tk, s2=None, op2=None):
                if op2 is None:
                    return C.dve(lambda e: e.tensor_scalar(out, a, s1, None, op), *tk)
                return C.dve(lambda e: e.tensor_scalar(out, a, s1, s2, op, op2), *tk)

            gm = alloc(4)
            t = RD(gm, G, ALU.max, t)
            eg = alloc(4, 4)
            gmb = gm.unsqueeze(2).broadcast_to([P, 4, 4])
            t = TT(eg, G, gmb, ALU.subtract, t)
            cand = alloc(4, 4)
            tc = TS(cand, eg, 0.0, ALU.is_equal, t)
            t_e = C.act(lambda e: e.activation(eg, eg, ACT.Exp), tc)
            rev4 = cs("rev4").unsqueeze(1).broadcast_to([P, 4, 4])
            t = TT(cand, cand, rev4, ALU.mult, tc)
            g1 = alloc(4)
            t = RD(g1, cand, ALU.max, t)
            ohg = alloc(4, 4)
            t = TT(ohg, rev4, g1.unsqueeze(2).broadcast_to([P, 4, 4]), ALU.is_equal, t)
            ohgb = ohg.unsqueeze(3).broadcast_to([P, 4, 4, 8])
            ml = alloc(4, 4, 8)
            t = TT(ml, L, ohgb, ALU.mult, t)
            ls = alloc(4, 8)
            t = RD(ls, ml.rearrange("p t g e -> p t e g"), ALU.add, t)
            rev8 = cs("rev8").unsqueeze(1).broadcast_to([P, 4, 8])
            ms, ohs = [], []
            for r in range(2):
                m = alloc(4)
                t = RD(m, ls, ALU.max, t)
                c8 = alloc(4, 8)
                t = TT(c8, ls, m.unsqueeze(2).broadcast_to([P, 4, 8]), ALU.is_equal, t)
                t = TT(c8, c8, rev8, ALU.mult, t)
                i1 = alloc(4)
                t = RD(i1, c8, ALU.max, t)
                oh = alloc(4, 8)
                t = TT(oh, rev8, i1.unsqueeze(2).broadcast_to([P, 4, 8]), ALU.is_equal, t)
                if r == 0:
                    t = C.dve(lambda e, oh=oh: e.scalar_tensor_tensor(ls, oh, -1e38, ls, ALU.mult, ALU.add), t)
                ms.append(m)
                ohs.append(oh)
            OH = []
            for r in range(2):
                o = alloc(4, 4, 8)
                t = TT(o, ohgb, ohs[r].unsqueeze(2).broadcast_to([P, 4, 4, 8]), ALU.mult, t)
                OH.append(o)
            oh = alloc(4, 4, 8)
            t = TT(oh, OH[0], OH[1], ALU.add, t)
            ohf = oh.rearrange("p t g e -> p t (g e)")
            ohf_flat = oh.rearrange("p t g e -> p (t g e)")
            b = bank()
            for i in range(NT):
                o = banks[b][:, 32 * i:32 * i + 32]
                for j in range(i + 1):
                    C.pe(lambda e, o=o, i=i, j=j: e.matmul(o, cs("tri") if j == i else ones, ohf[:, j, :], start=(j == 0), stop=(j == i)),
                         t, *bank_free[b], inc=False)
            for j in range(NT):
                tp = C.pe(lambda e, j=j: e.matmul(banks[b][:, 128:160], ones, ohf[:, j, :], start=(j == 0), stop=(j == 3)), inc=(j == 3))
            rc = alloc(160)
            t = C.dve(lambda e: e.tensor_copy(rc, banks[b][:, 0:160]), tp)
            bank_free[b] = [t]
            rk = rc[:, 0:128]
            cnt = rc[:, 128:160]
            t_rc = t
            ps = alloc(128)
            t = C.dve(lambda e: e.scalar_tensor_tensor(ps, rk, 1.0, ohf_flat, ALU.add, ALU.mult), t)
            t_ps = TS(ps, ps, -1.0, ALU.add, t)
            place = ps.rearrange("p (t e) -> p t e", t=NT)
            sel = alloc(2 * NT, 2 * CAP)
            out_ = {}
            pos_i = posi[l]
            wt = small[:, 8 + 8 * l:16 + 8 * l]

            def rest():
                t = t_rc
                sg = alloc(4)
                t = RD(sg, eg, ALU.add, t_rc, t_e)
                d2 = alloc(4)
                t = TT(d2, ms[1], ms[0], ALU.subtract, t)
                t = C.act(lambda e: e.activation(d2, d2, ACT.Exp), t)
                q2 = alloc(4)
                t = TS(q2, d2, 1.0, ALU.add, t)
                t = TT(q2, q2, sg, ALU.mult, t)
                t = C.dve(lambda e: e.reciprocal(wt[:, 0:4], q2), t)
                t = TT(wt[:, 4:8], wt[:, 0:4], d2, ALU.mult, t)
                nx = alloc(32)
                t = TS(nx, cnt, float(CAP), ALU.is_gt, t)
                tmp32 = alloc(32)
                for j in range(2, S // CAP):
                    t = TS(tmp32, cnt, float(j * CAP), ALU.is_gt, t)
                    t = TT(nx, nx, tmp32, ALU.add, t)
                cum = alloc(32)
                one32 = ones[:, 0:32]
                t = C.dve(lambda e: e.tensor_tensor_scan(cum, one32, nx, 0.0, ALU.mult, ALU.add), t)
                base = alloc(32)
                t = TT(base, cum, nx, ALU.subtract, t)
                t = TT(base, base, cs("iota32"), ALU.subtract, t)
                t = TS(base, base, 32.0, ALU.add, t)
                yield
                q = alloc(128)
                t = TS(q, rk, float(CAP), ALU.is_ge, t)
                ex = alloc(4, 32)
                t = TT(ex, q.rearrange("p (t e) -> p t e", t=4), base.unsqueeze(1).broadcast_to([P, 4, 32]), ALU.mult, t)
                t = TT(ex, ex, cs("iota32").unsqueeze(1).broadcast_to([P, 4, 32]), ALU.add, t)
                tq = alloc(128)
                for j in range(2, S // CAP):
                    t = TS(tq, rk, float(j * CAP), ALU.is_ge, t)
                    t = TT(q, q, tq, ALU.add, t)
                yield
                sf = alloc(128)
                t = C.dve(lambda e: e.scalar_tensor_tensor(sf, q, float(-CAP), rk, ALU.mult, ALU.add), t)
                bf = alloc(128)
                qm = alloc(128)
                t = TS(qm, q, -1.0, ALU.add, t, s2=0.0, op2=ALU.max)
                t = TT(bf, qm, ex.rearrange("p t e -> p (t e)"), ALU.add, t)
                sb_ = []
                for r in range(2):
                    yield
                    mp = alloc(4, 32)
                    t = TT(mp, OH[r].rearrange("p t g e -> p t (g e)"), sf.rearrange("p (t e) -> p t e", t=4), ALU.mult, t)
                    sr = alloc(4)
                    t = RD(sr, mp, ALU.add, t)
                    t = TT(mp, OH[r].rearrange("p t g e -> p t (g e)"), bf.rearrange("p (t e) -> p t e", t=4), ALU.mult, t)
                    br_ = alloc(4)
                    t = RD(br_, mp, ALU.add, t)
                    pr = alloc(4)
                    t = C.dve(lambda e, pr=pr, sr=sr, br_=br_: e.scalar_tensor_tensor(pr, sr, float(NB), br_, ALU.mult, ALU.add), t)
                    t = C.dve(lambda e, r=r, pr=pr: e.tensor_copy(pos_i[:, 4 * r:4 * r + 4], pr), t)
                    sb_.append((sr, br_))
                cmpb = alloc(NOVF, 32)
                t = TT(cmpb, cum.unsqueeze(1).broadcast_to([P, NOVF, 32]), cs("iotab").unsqueeze(2).broadcast_to([P, NOVF, 32]), ALU.is_le, t)
                eo = alloc(NOVF)
                t = RD(eo, cmpb, ALU.add, t)
                t = TS(eo, eo, float(NE - 1), ALU.min, t)
                C.dve(lambda e: e.tensor_copy(ovf_i[l][:, 0:NOVF], eo), t)
                out_["ovf"] = C.dve(lambda e: e.tensor_copy(ovf_i[l][:, NOVF:NOVF + 1], cum[:, 31:32]), t)
                one_s = alloc(8, CAP)
                one_b = alloc(8, NB)
                ones_t = []
                for r in range(2):
                    yield
                    for i in range(NT):
                        m_ = 4 * r + i
                        sr, br_ = sb_[r]
                        t1 = C.dve(lambda e, m_=m_, i=i, sr=sr: e.tensor_scalar(one_s[:, m_, :], cs("iotas"), sr[:, i:i + 1], None, ALU.is_equal), t)
                        t2 = C.dve(lambda e, m_=m_, i=i, br_=br_: e.tensor_scalar(one_b[:, m_, :], cs("iotas")[:, 0:NB], br_[:, i:i + 1], cs("tok")[:, i:i + 1], ALU.is_equal, ALU.mult), t)
                        ones_t.append((t1, t2))
                yield
                bq = bank()
                for m_ in range(8):
                    tp = C.pe(lambda e, m_=m_: e.matmul(banks[bq][0:CAP, 0:NB], one_s[:, m_, :], one_b[:, m_, :], start=(m_ == 0), stop=(m_ == 7)),
                              *ones_t[m_], *bank_free[bq])
                yield
                out_["ix"] = C.dve(lambda e: e.tensor_copy(idx[0:CAP, :], banks[bq][0:CAP, 0:NB]), tp)
                bank_free[bq] = [out_["ix"]]
                assert so[0] <= 16384


            o = 0
            xe = ar(o, 1024)
            xeT = ar(o + 1024, 4 * KT * CAP).rearrange("p (b k c) -> p b k c", b=2, k=KT)
            o += 1024 + 4 * KT * CAP
            sl = ar(o, 1024).rearrange("p (b d) -> p b d", b=2)
            hh = ar(o + 1024, 1024).rearrange("p (b d) -> p b d", b=2)
            hT = ar(o + 2048, 2 * 4 * CAP).rearrange("p (b k c) -> p b k c", b=2, k=4)
            o += 2048 + 8 * CAP
            yy = ar(o, 2048).rearrange("p (b d) -> p b d", b=2)
            o += 2048
            l_ys = [Lane(nc, ctx, f"l_ys{l}_{i}") for i in range(2)]
            entry = [C.last("pe"), C.last("dve"), C.last("act")]
            xr = ar(16384, 4096).rearrange("p (t d) -> p t d", t=NT)
            sel_t, free_sel, xT_t, free_xeT = {}, {}, {}, {}
            hh_t, hT_t, free_hh, free_hT, free_sl, y_free, ys_t = {}, {}, {}, {}, {}, {}, {}

            def SEL(p_):
                j = p_ % 2
                for i in range(NT):
                    for z in range(2):
                        t = C.dve(lambda e, i=i, z=z: e.tensor_scalar(sel[:, NT * j + i, z * CAP:(z + 1) * CAP], cs("iotas"),
                                                                      place[:, i, 2 * p_ + z:2 * p_ + z + 1], None, ALU.is_equal),
                                  t_ps, *free_sel.get(p_ - 2, []))
                sel_t[p_] = t

            def XT(p_, q_):
                j = p_ % 2
                b = bank()
                for k in range(4):
                    kk = 4 * q_ + k
                    for i in range(NT):
                        t = C.pe(lambda e, k=k, kk=kk, i=i: e.matmul(banks[b][:, k * P:(k + 1) * P], xr[:, i, kk * P:(kk + 1) * P], sel[:, NT * j + i, :],
                                                                    start=(i == 0), stop=(i == NT - 1)),
                                 sel_t[p_], *bank_free[b], inc=(k == 3 and i == NT - 1))
                tt = C.dve(lambda e: e.tensor_copy(xeT[:, j, 4 * q_:4 * q_ + 4, :], banks[b][:].rearrange("p (k c) -> p k c", k=4)),
                           t, *free_xeT.get(p_ - 2, []), *entry)
                bank_free[b] = [tt]
                free_sel[p_] = [t]
                xT_t.setdefault(p_, []).append(tt)

            def GU(e_):
                j = e_ % 2
                us = [load(t_["wexp"][l, e_, m_]) for m_ in range(2)]
                ws = [u.ap.rearrange("p (k n) -> p k n", k=KT) for u in us]
                bs = [bank(), bank()]
                outs = [banks[bs[0]][0:CAP, :], banks[bs[1]][64:64 + CAP, :]]
                for k in range(KT):
                    for m_ in range(2):
                        t = C.pe(lambda e, k=k, m_=m_: e.matmul(outs[m_], xeT[:, e_ // 2 % 2, k, e_ % 2 * CAP:(e_ % 2 + 1) * CAP], ws[m_][:, k, :], start=(k == 0), stop=(k == KT - 1)),
                                 us[m_].tok, *bank_free[bs[m_]], *xT_t[e_ // 2], inc=(k == KT - 1 and m_ == 1))
                ts = [t, t]
                for u in us:
                    release(u, t)
                free_xeT[e_ // 2] = [ts[1]]
                t = C.act(lambda e: e.activation(sl[0:CAP, j, :], banks[bs[0]][0:CAP, :], ACT.Silu), ts[0], *free_sl.get(e_ - 2, []), *entry)
                bank_free[bs[0]] = [t]
                t = C.dve(lambda e: e.tensor_tensor(hh[0:CAP, j, :], sl[0:CAP, j, :], banks[bs[1]][64:64 + CAP, :], ALU.mult), t, ts[1], *free_hh.get(e_ - 2, []))
                bank_free[bs[1]] = [t]
                free_sl[e_] = [t]
                hh_t[e_] = t

            def HT(e_):
                j = e_ % 2
                b = bank()
                for k in range(4):
                    t = C.pe(lambda e, k=k: e.transpose(banks[b][:, k * CAP:(k + 1) * CAP], hh[0:CAP, j, k * P:(k + 1) * P], ident[0:CAP, 0:CAP]),
                             hh_t[e_], *bank_free[b], inc=(k == 3))
                free_hh[e_] = [t]
                t = C.act(lambda e: e.activation(hT[:, j, :, :], banks[b][:, 0:4 * CAP].rearrange("p (k c) -> p k c", k=4), ACT.Copy),
                          t, *free_hT.get(e_ - 2, []), *entry)
                bank_free[b] = [t]
                hT_t[e_] = t

            def DOWN(e_):
                j = e_ % 2
                u = load(t_["wexp"][l, e_, 2])
                w = u.ap.rearrange("p (k n) -> p k n", k=4)
                bs = [bank(), bank()]
                outs = [banks[bs[0]][0:CAP, :], banks[bs[1]][64:64 + CAP, :]]
                for k in range(4):
                    for c in range(2):
                        t = C.pe(lambda e, k=k, c=c: e.matmul(outs[c], hT[:, j, k, :], w[:, k, c * 512:(c + 1) * 512], start=(k == 0), stop=(k == 3)),
                                 u.tok, *bank_free[bs[c]], hT_t[e_], inc=(k == 3 and c == 1))
                ta = C.act(lambda e: e.activation(yy[0:CAP, j, 0:512], outs[0], ACT.Copy), t, *y_free.get(e_ - 2, []), *entry)
                tb = C.dve(lambda e: e.tensor_copy(yy[0:CAP, j, 512:1024], outs[1]), t, *y_free.get(e_ - 2, []), *entry)
                bank_free[bs[0]], bank_free[bs[1]] = [ta], [tb]
                out = [ta, tb]
                release(u, t)
                free_hT[e_] = [t]
                ys_t[e_] = l_ys[j].dma(C, "pool", lambda e: e.dma_start(y_d[l].rearrange("(s b) d -> b s d", b=NB)[e_], yy[0:CAP, j, :]), *out)
                y_free[e_] = [ys_t[e_]]

            SEL(0)
            SEL(1)
            XT(0, 0)
            XT(0, 1)
            more = rest()
            for e_ in range(NE):
                GU(e_)
                if e_ % 2 == 0 and e_ // 2 + 2 < NE // 2:
                    SEL(e_ // 2 + 2)
                if e_ >= 1:
                    DOWN(e_ - 1)
                if e_ // 2 + 1 < NE // 2:
                    XT(e_ // 2 + 1, e_ % 2)
                next(more, None)
                HT(e_)
                if e_ == NE // 2:
                    t_p = l_p[l].dma(C, "pool", lambda e: e.dma_start(ar(10240, 1024), t_["pT"][l]), *entry, out_["ix"])
                    t_p = l_p[l].dma(C, "pool", lambda e: e.dma_start(ar(11264, 1024)[0:1, :], t_["plebias"][l:l + 1, :]), *entry, out_["ix"])
            DOWN(NE - 1)
            assert "ix" in out_ and next(more, None) is None
            t_ovf = out_["ovf"]

            main = [cy_t[l], *xs_t, out_["ix"], C.last("pe"), C.last("act"), C.last("dve"), ys_t[NE - 1], ys_t[NE - 2], t_ovf]
            O = Core(nc, ctx, f"o{l}", engines=("pe", "act", "dve"))
            lw = Lane(nc, ctx, f"lw{l}")
            lo = Lane(nc, ctx, f"lo{l}")
            lists = {e: [] for e in C.q}
            prev = []
            for bk in range(NOVF):
                q0 = {e: [] for e in C.q}
                O.q = q0
                O.seen = {e: {} for e in C.q}
                for e in C.q:
                    O.wait(e, *main, *prev)
                for m_ in range(3):
                    tw = lw.dma(O, "sp", lambda e, m_=m_: e.dma_start(ring[:, m_ * UNIT:(m_ + 1) * UNIT], t_["wexp"][l, bass.DynSlice(eo_box[0], 1), m_].rearrange("a p n -> (a p) n")))
                tg = lo.dma(O, "pool", lambda e, bk=bk: e.indirect_dma_start(
                    out=xe[0:CAP, :], out_offset=None, in_=xs_d[l],
                    in_offset=bass.IndirectOffsetOnAxis(ap=idx[0:CAP, NE + bk:NE + bk + 1], axis=0)))
                ev = []
                for q_ in range(KT * CAP // 512):
                    per = 512 // CAP
                    for k in range(per):
                        kk = q_ * per + k
                        t = O.pe(lambda e, q_=q_, k=k, kk=kk: e.transpose(banks[q_][:, k * CAP:(k + 1) * CAP], xe[0:CAP, kk * P:(kk + 1) * P], ident[0:CAP, 0:CAP]), tg)
                    ev.append(O.dve(lambda e, q_=q_, per=per: e.tensor_copy(xeT[:, 0, q_ * per:(q_ + 1) * per, 0:CAP], banks[q_][:].rearrange("p (k c) -> p k c", k=per)), t))
                for m_ in range(2):
                    w = ring[:, m_ * UNIT:(m_ + 1) * UNIT].rearrange("p (k n) -> p k n", k=KT)
                    for k in range(KT):
                        t = O.pe(lambda e, m_=m_, k=k, w=w: e.matmul(banks[2 + m_][0:CAP, :], xeT[:, 0, k, 0:CAP], w[:, k, :], start=(k == 0), stop=(k == 7)), tw, *ev)
                t = O.act(lambda e: e.activation(sl[0:CAP, 0, :], banks[2][0:CAP, :], ACT.Silu), t)
                t = O.dve(lambda e: e.tensor_tensor(hh[0:CAP, 0, :], sl[0:CAP, 0, :], banks[3][0:CAP, :], ALU.mult), t)
                for k in range(4):
                    t2 = O.pe(lambda e, k=k: e.transpose(banks[4][:, k * CAP:(k + 1) * CAP], hh[0:CAP, 0, k * P:(k + 1) * P], ident[0:CAP, 0:CAP]), t)
                t = O.act(lambda e: e.activation(hT[:, 0, :, :], banks[4][:, 0:4 * CAP].rearrange("p (k c) -> p k c", k=4), ACT.Copy), t2)
                w = ring[:, 2 * UNIT:3 * UNIT].rearrange("p (k n) -> p k n", k=4)
                for c in range(2):
                    for k in range(4):
                        t3 = O.pe(lambda e, c=c, k=k, w=w: e.matmul(banks[5 + c][0:CAP, :], hT[:, 0, k, :], w[:, k, c * 512:(c + 1) * 512], start=(k == 0), stop=(k == 3)), t)
                ta = O.act(lambda e: e.activation(yy[0:CAP, 0, 0:512], banks[5][0:CAP, :], ACT.Copy), t3)
                tb = O.dve(lambda e: e.tensor_copy(yy[0:CAP, 0, 512:1024], banks[6][0:CAP, :]), t3)
                ty = lo.dma(O, "pool", lambda e, bk=bk: e.dma_start(y_d[l].rearrange("(s b) d -> b s d", b=NB)[NE + bk], yy[0:CAP, 0, :]), ta, tb)
                for e in C.q:
                    O.wait(e, ty)
                    lists[e].append(q0[e])
                prev = [ty]

            def emit(e, steps, name, l=l):
                nv = e.value_load(ovf_i[l][0:1, NOVF:NOVF + 1], min_val=0, max_val=NOVF)

                def rec(bk):
                    if bk == len(steps):
                        return
                    with e.If(nv > bk):
                        if name == "sp":
                            eo_box[0] = e.value_load(ovf_i[l][0:1, bk:bk + 1], min_val=0, max_val=NE - 1)
                        for f in steps[bk]:
                            f(e)
                        rec(bk + 1)
                rec(0)

            for e in C.q:
                C.wait(e, t_ovf)
                C.q[e].append(lambda en, e=e: emit(en, lists[e], e))

            yg = [ar(o_, D) for o_ in (12288, 13312, 14336, 15360, 20480, 21504, 22528, 8704)]
            l_yg = [Lane(nc, ctx, f"l_yg{l}_{i}") for i in range(2 * NT)]
            ready = [ys_t[NE - 1], ys_t[NE - 2], cy_t[l], C.last("dve"), C.last("act")]
            tk = {}

            def fetch(i):
                for r in range(2):
                    j = 2 * i + r
                    tk[(i, r)] = l_yg[j].dma(C, "pool", lambda e, r=r, j=j: e.indirect_dma_start(
                        out=yg[j], out_offset=None, in_=y_d[l],
                        in_offset=bass.IndirectOffsetOnAxis(ap=pos_i[:, 4 * r + i:4 * r + i + 1], axis=0)),
                        *ready)

            for i in range(NT):
                fetch(i)
            pT = ar(10240, 1024).rearrange("p (k s) -> p k s", k=2)
            PP = ar(16384, 4096).rearrange("p (t c) -> p t c", t=NT)
            up = load(wnext()[:, 0:2048], 2048)
            wp = up.ap.rearrange("p (k n) -> p k n", k=2)
            for i in range(NT):
                for c in range(2):
                    b2 = bank()
                    t2 = mm_group(banks[b2][:], [(pT[:, k, i * P:(i + 1) * P], wp[:, k, 512 * c:512 * c + 512]) for k in range(2)], True,
                                  up.tok, t_p, *bank_free[b2])
                    t = C.act(lambda e, b2=b2, i=i, c=c: e.activation(PP[:, i, 512 * c:512 * c + 512], banks[b2][:], ACT.Copy), t2, *entry)
                    bank_free[b2] = [t]
            release(up, t2)
            for i in range(NT):
                for r in range(2):
                    j = 2 * i + r
                    t = C.dve(lambda e, i=i, r=r, j=j: e.scalar_tensor_tensor(
                        h[:, i, :], yg[j], wt[:, 4 * r + i:4 * r + i + 1], h[:, i, :], ALU.mult, ALU.add), tk[(i, r)], *h_tok[i])
                    h_tok[i] = [t]
                nxt.feed(i)
                nxt.behind(i)
            nxt.finish()

        eo_box = [None]
        posi = [sb(f"posi{l}", [P, 8], I32) for l in range(2)]
        ovf_i = [sb(f"ovfi{l}", [P, NOVF + 1], I32) for l in range(2)]
        idx = sb("idx", [P, NB], I32)
        l_p = [Lane(nc, ctx, f"l_p{l}") for l in range(2)]

        def ple(l, N, nxt):
            xT, res = N.xT, N.res
            br = ar(11264, 1024)
            PP = ar(16384, 4096).rearrange("p (t c) -> p t c", t=NT)
            t_p = (l_p[l].sem, l_p[l].n)
            sg = ar(8192, 2048).rearrange("p (b s) -> p b s", b=4)
            entry = [C.last("pe"), C.last("dve"), C.last("act")]
            fr = {}
            c_ = 0
            for c in range(2):
                u = load(wnext())
                w = u.ap.rearrange("p (k n) -> p k n", k=KT)
                for i in range(NT):
                    j = c_ % 4
                    b = bank()
                    C.pe(lambda e, b=b, c=c: e.matmul(banks[b][:], ones[0:1, :], br[0:1, 512 * c:512 * c + 512], start=True, stop=False),
                         t_p, *bank_free[b], inc=False)
                    for k in range(KT):
                        t = C.pe(lambda e, b=b, k=k, i=i, w=w: e.matmul(banks[b][:], xT[:, k, i * P:(i + 1) * P], w[:, k, :], start=False, stop=(k == 7)),
                                 u.tok, *res[i], inc=(k == 7))
                    if i == NT - 1:
                        release(u, t)
                    t = C.act(lambda e, b=b, j=j: e.activation(sg[:, j, :], banks[b][:], ACT.Sigmoid), t, *fr.get(c_ - 4, []), *entry)
                    bank_free[b] = [t]
                    t = C.dve(lambda e, i=i, c=c, j=j: e.tensor_tensor(sg[:, j, :], sg[:, j, :], PP[:, i, 512 * c:512 * c + 512], ALU.mult), t)
                    t = C.dve(lambda e, i=i, c=c, j=j: e.tensor_tensor(h[:, i, 512 * c:512 * c + 512], h[:, i, 512 * c:512 * c + 512], sg[:, j, :], ALU.add), t, *h_tok[i])
                    fr[c_] = [t]
                    h_tok[i] = [t]
                    if c == 1:
                        nxt.feed(i)
                        nxt.behind(i)
                    c_ += 1
            nxt.finish()

        def mixer_b(N, nxt):
            xT = ar(0, 4096).rearrange("p (k s) -> p k s", k=KT)
            yT = ar(4096, 4096).rearrange("p (k s) -> p k s", k=KT)
            uc = ar(8192, 4096).rearrange("p (k s) -> p k s", k=KT)
            hs = ar(12288, 4096).rearrange("p (k s) -> p k s", k=KT)
            entry = [C.last("pe"), C.last("dve"), C.last("act"), *cy_t]
            xt = [t for r in N.res.values() for t in r]
            up = ar(22528, 1032).rearrange("p (b s) -> p b s", b=2)
            tz = C.dve(lambda e: e.memset(up, 0.0), *entry)
            cb = cs("convb").rearrange("p (c k) -> p c k", c=8)
            fr, uct, yt = {}, {}, {}
            def project(q):
                u = load(wnext())
                w = u.ap.rearrange("p (k n) -> p k n", k=KT)
                for c4 in range(4):
                    b = bank()
                    t = mm_group(banks[b][:], [(w[:, k, c4 * P:(c4 + 1) * P], xT[:, k, :]) for k in range(KT)], True,
                                 u.tok, *bank_free[b], *xt)
                    c = 4 * (q % 2) + c4
                    if q >= 2:
                        t = C.act(lambda e, b=b, c=c: e.activation(yT[:, c, :], banks[b][:], ACT.Gelu_apprx_tanh), t, *entry)
                        bank_free[b] = [t]
                        yt[c] = t
                    else:
                        j = c % 2
                        t = C.act(lambda e, b=b, j=j: e.activation(up[:, j, 2:514], banks[b][:], ACT.Copy), t, tz, *fr.get(c - 2, []))
                        bank_free[b] = [t]
                        t = C.dve(lambda e, j=j, c=c: e.tensor_scalar(uc[:, c, :], up[:, j, 0:512], cb[:, c, 0:1], cs("cbias")[:, c:c + 1], ALU.mult, ALU.add), t, *entry)
                        for m in range(1, 4):
                            t = C.dve(lambda e, j=j, c=c, m=m: e.scalar_tensor_tensor(uc[:, c, :], up[:, j, m:m + 512], cb[:, c, m:m + 1], uc[:, c, :], ALU.mult, ALU.add), t)
                        fr[c] = [t]
                        uct[c] = t
                release(u, C.last("pe"))
            project(0)
            project(1)
            Rs = [ar(16384, 2048).rearrange("p (k s) -> p k s", k=4), None]
            Is = [ar(18432, 2048).rearrange("p (k s) -> p k s", k=4), None]
            T_ = ar(20480, 2048).rearrange("p (k s) -> p k s", k=4)
            frt = [C.last("dve"), C.last("pe")]
            frs = [frt, frt]
            hst = {}
            for d in range(2):
                u = load(wnext())
                if d == 0:
                    scratch = reserve()
                    Rs[1], Is[1] = (scratch.ap[:, 2048 * z:2048 * z + 2048].rearrange("p (k s) -> p k s", k=4) for z in range(2))
                    frs[1] = frt + scratch.free
                w = u.ap.rearrange("p (a b k n) -> p a b k n", a=2, b=4, k=2)
                for hf in range(2):
                    R_, I_ = Rs[hf], Is[hf]
                    tr, ti = {}, {}
                    for cc in range(4):
                        c = 4 * hf + cc
                        blk, m = c // 2, c % 2
                        for a, (dst, bn, td) in enumerate(((R_, "br", tr), (I_, "bi", ti))):
                            b = bank()
                            t = mm_group(banks[b][:], [(w[:, a, blk, k, m * P:(m + 1) * P], uc[:, 2 * blk + k, :]) for k in range(2)], True,
                                         u.tok, *bank_free[b], uct[2 * blk], uct[2 * blk + 1])
                            t = C.act(lambda e, b=b, dst=dst, cc=cc, c=c, bn=bn, d=d: e.activation(
                                dst[:, cc, :], banks[b][:], ACT.Sigmoid, bias=cs(bn)[:, 8 * d + c:8 * d + c + 1]), t, *frs[hf])
                            bank_free[b] = [t]
                            td[cc] = t
                    tT, tA, tI_, tM = {}, {}, {}, {}
                    for cc in range(4):
                        c = 4 * hf + cc
                        sp_ = nspt[:, 8 * d + c:8 * d + c + 1]
                        tT[cc] = C.act(lambda e, cc=cc, sp_=sp_, R_=R_: e.activation(T_[:, cc, :], R_[:, cc, :], ACT.Tanh, scale=sp_), tr[cc], *nsp_tok, *frt)
                        tA[cc] = C.act(lambda e, cc=cc, sp_=sp_, R_=R_: e.activation(R_[:, cc, :], R_[:, cc, :], ACT.Exp, scale=sp_), tT[cc])
                        tI_[cc] = C.pool(lambda e, cc=cc, c=c, I_=I_: e.tensor_tensor(I_[:, cc, :], I_[:, cc, :], uc[:, c, :], ALU.mult), ti[cc])
                        x1 = up[:, cc % 2, 0:512]
                        t = C.dve(lambda e, cc=cc, x1=x1, R_=R_: e.tensor_tensor(x1, R_[:, cc, :], R_[:, cc, :], ALU.mult), tA[cc], C.last("dve"))
                        tM[cc] = C.dve(lambda e, cc=cc, x1=x1: e.scalar_tensor_tensor(T_[:, cc, :], x1, 1.0, T_[:, cc, :], ALU.add, ALU.mult), t)
                    for cc in range(4):
                        c = 4 * hf + cc
                        t = C.act(lambda e, cc=cc: e.activation(T_[:, cc, :], T_[:, cc, :], ACT.Sqrt, scale=-1.0, bias=tiny[:, 0:1]), tM[cc])
                        t = C.dve(lambda e, cc=cc, I_=I_: e.tensor_tensor(I_[:, cc, :], I_[:, cc, :], T_[:, cc, :], ALU.mult), t, tI_[cc])
                        if d == 0:
                            t = C.dve(lambda e, cc=cc, c=c, R_=R_, I_=I_: e.tensor_tensor_scan(hs[:, c, :], R_[:, cc, :], I_[:, cc, :], 0.0, ALU.mult, ALU.add), t)
                            hst[c] = t
                        else:
                            t = C.dve(lambda e, cc=cc, R_=R_, I_=I_: e.tensor_tensor_scan(T_[:, cc, ::-1], R_[:, cc, ::-1], I_[:, cc, ::-1], 0.0, ALU.mult, ALU.add), t)
                            t = C.pool(lambda e, cc=cc, c=c: e.tensor_tensor(hs[:, c, :], hs[:, c, :], T_[:, cc, :], ALU.add), t, hst[c])
                            hst[c] = t
                        last = t
                    frt = [last]
                    frs[hf] = [last, C.last("dve")]
                release(u, C.last("pe"))
                project(2 + d)
            for c in range(8):
                last = C.pool(lambda e, c=c: e.tensor_tensor(yT[:, c, :], yT[:, c, :], hs[:, c, :], ALU.mult), hst[c], yt[c])
            release(scratch, C.last("dve"), C.last("pool"), C.last("pe"))
            out_proj(yT, [last], [wnext(), wnext()], nxt)

        def attention(N):
            xT = ar(0, 4096).rearrange("p (k s) -> p k s", k=KT)
            QK = ar(4096, 8704).rearrange("p (j s) -> p j s", j=17)
            V = ar(12800, 1536).rearrange("p (t c) -> p t c", t=NT)
            A = ar(14336, 2048).rearrange("p (j s) -> p j s", j=4)
            Z = ar(16384, 4096).rearrange("p (t c) -> p t c", t=NT)
            GT = ar(20480, 112).rearrange("p (t c) -> p t c", t=NT)
            DMo = 20592
            Wk = 21744
            res = N.res
            gf = gbuf[:].rearrange("p b d -> p (b d)")
            hg, hgc = gf[:, 0:HG], gf[:, HG - 128:HG]
            ksq2 = gf[:, 1536:1664]
            mx8 = gf[:, 1664:1696].rearrange("p (t c) -> p t c", t=NT)
            l_hg = Lane(nc, ctx, "l_hg")
            t_hg = l_hg.dma(C, "pool", lambda e: e.dma_start(hg, t_["hgain"].broadcast_to([P, HG])), C.last("dve"))
            entry = [C.last("pe"), C.last("dve"), C.last("act")]
            cosb = cs("cos").rearrange("p (t c) -> p t c", t=NT)
            sinb = cs("sin").rearrange("p (t c) -> p t c", t=NT)
            stg = ar(16384, 4096).rearrange("p (b c) -> p b c", b=2)
            t2b = ar(Wk, 512)
            pend = {}
            ssq = small[:, 24:56]
            qkt = {}
            cnt = [0]

            def rope_block(src, dst, nh, cos, sin, tmp, rows, *tk):
                def hv(a, half):
                    return a.rearrange("p (n c) -> p n c", c=64)[:, :, 32 * half:32 * half + 32]
                cb = cos.unsqueeze(1).broadcast_to([rows, nh, 32])
                sbb = sin.unsqueeze(1).broadcast_to([rows, nh, 32])
                s1, s2, d1, d2 = hv(src, 0), hv(src, 1), hv(dst, 0), hv(dst, 1)
                u1, u2 = hv(tmp, 0), hv(tmp, 1)
                a = C.dve(lambda e: e.tensor_tensor(d1, s1, cb, ALU.mult), *tk)
                b = C.dve(lambda e: e.tensor_tensor(u1, s2, sbb, ALU.mult), *tk)
                c = C.dve(lambda e: e.tensor_tensor(d2, s2, cb, ALU.mult), *tk)
                d = C.dve(lambda e: e.tensor_tensor(u2, s1, sbb, ALU.mult), *tk)
                C.dve(lambda e: e.tensor_tensor(d1, d1, u1, ALU.subtract), a, b)
                return C.dve(lambda e: e.tensor_tensor(d2, d2, u2, ALU.add), c, d)

            def head_norm(x, sq, gain, nh, rows, ss, *tk):
                x3 = x.rearrange("p (n c) -> p n c", c=64)
                t = C.dve(lambda e: e.tensor_tensor(sq, x, x, ALU.mult), *tk)
                t = C.dve(lambda e: e.tensor_reduce(ss, sq.rearrange("p (n c) -> p n c", c=64), X, ALU.add), t)
                t = C.dve(lambda e: e.tensor_scalar(ss, ss, 1.0 / 64, EPS, ALU.mult, ALU.add), t)
                t = C.act(lambda e: e.activation(ss, ss, ACT.Sqrt), t)
                t = C.dve(lambda e: e.reciprocal(ss, ss), t)
                t = C.dve(lambda e: e.tensor_tensor(x3, x3, ss.unsqueeze(2).broadcast_to([rows, nh, 64]), ALU.mult), t)
                return C.dve(lambda e: e.tensor_tensor(x, x, gain, ALU.mult), t)

            queue = []

            def flush(keep):
                while len(queue) > keep:
                    queue.pop(0)()

            def transposes(src, npair, toks, key, i, dest, fin):
                def go():
                    b0 = 0
                    while b0 < npair:
                        m = min(4, npair - b0)
                        b = bank()
                        for k in range(m):
                            s_ = src(b0 + k)
                            t = C.pe(lambda e, b=b, k=k, s_=s_: e.transpose(banks[b][:, k * P:(k + 1) * P], s_, ident), *toks, *bank_free[b], inc=(k == m - 1))
                        t = C.act(lambda e, b=b, m=m, b0=b0: e.activation(dest(b0, m), banks[b][:, 0:m * P].rearrange("p (k c) -> p k c", k=m), ACT.Copy), t, *entry)
                        bank_free[b] = [t]
                        b0 += m
                    fin(t)
                queue.append(go)

            specs = [
                (8, True, 0, 8, 0), (8, True, 4, 8, 512), (6, True, 8, 0, 1024), (5, False, 14, 4, None)]
            stg_free = {}
            for c, (nh, normed, pair0, dbl, goff) in enumerate(specs):
                n = nh * 64
                u = load(wnext()[:, 0:8 * n], 8 * n)
                w = u.ap.rearrange("p (k n) -> p k n", k=KT)
                for i in range(NT):
                    j = cnt[0] % 2
                    b = bank()
                    t = mm_group(banks[b][:, 0:n], [(xT[:, k, i * P:(i + 1) * P], w[:, k, :]) for k in range(KT)], True,
                                 u.tok, *bank_free[b], *res[i])
                    pr, sq, ro = stg[:, j, 0:n], stg[:, j, 512:512 + n], stg[:, j, 1024:1024 + n]
                    fr = stg_free.get(cnt[0] - 2, entry)
                    t = C.act(lambda e, b=b, pr=pr, n=n: e.activation(pr, banks[b][:, 0:n], ACT.Copy), t, *fr, *entry)
                    bank_free[b] = [t]
                    if normed:
                        t = head_norm(pr, sq, hg[:, goff:goff + n], nh, P, ssq[:, 0:nh], t, t_hg, *fr)
                    t = rope_block(pr, ro, nh, cosb[:, i, :], sinb[:, i, :], sq, P, t, *fr)
                    if dbl >= nh:
                        src = lambda k, ro=ro: ro[:, k * P:(k + 1) * P]
                        npair = nh // 2
                    else:
                        npair = (2 * nh - dbl) // 2
                        du = stg[:, j, 0:1024] if nh == 6 else stg[:, j, 512:1024]
                        if nh == 6:
                            r3 = ro.rearrange("p (n c) -> p n c", c=64)
                            d4 = stg[:, j, 0:768].rearrange("p (n r c) -> p n r c", n=6, r=2)
                            C.dve(lambda e, d4=d4, r3=r3: e.tensor_copy(d4[:, :, 0, :], r3), t)
                            t = C.dve(lambda e, d4=d4, r3=r3: e.tensor_copy(d4[:, :, 1, :], r3), t)
                            src = lambda k, j=j: stg[:, j, k * P:(k + 1) * P]
                        else:
                            t = C.dve(lambda e, j=j: e.tensor_copy(stg[:, j, 1344:1408], stg[:, j, 1280:1344]), t)
                            src = lambda k, ro=ro, j=j: stg[:, j, 1024 + k * P:1024 + (k + 1) * P]

                    def fin(t, n_=cnt[0], c=c, i=i):
                        stg_free[n_] = [C.last("pe")]
                        qkt[(c, i)] = t
                    flush(0)
                    transposes(src, npair, [t], c, i, lambda b0, m, i=i, pair0=pair0: QK[:, pair0 + b0:pair0 + b0 + m, i * P:(i + 1) * P], fin)
                    cnt[0] += 1
                release(u, C.last("pe"))
                flush(0) if c == 3 else None
                if c < 3:
                    flush(0)
            u = load(wnext()[:, 0:8 * 284], 8 * 284)
            w = u.ap.rearrange("p (k n) -> p k n", k=KT)
            at = {}
            gate_t = {}
            tz = C.dve(lambda e: e.memset(A[64:128, :, 511:512], 0.0), *entry)
            for i in range(NT):
                j = cnt[0] % 2
                b = bank()
                t0 = mm_group(banks[b][:, 0:284], [(xT[:, k, i * P:(i + 1) * P], w[:, k, :]) for k in range(KT)], True,
                              u.tok, *bank_free[b], *res[i])
                fr = stg_free.get(cnt[0] - 2, entry)
                kv = stg[:, j, 0:512].rearrange("p (n r c) -> p n r c", n=4, r=2)
                pv = banks[b][:, 0:256].rearrange("p (n c) -> p n c", c=64)
                ta = C.act(lambda e, kv=kv, pv=pv: e.activation(kv[:, :, 0, :], pv, ACT.Copy), t0, *fr)
                tb = C.act(lambda e, kv=kv, pv=pv: e.activation(kv[:, :, 1, :], pv, ACT.Copy), t0, *fr)
                t1 = C.act(lambda e, b=b, i=i: e.activation(GT[:, i, 0:24], banks[b][:, 256:280], ACT.Sigmoid), t0, *entry)
                t2 = C.act(lambda e, b=b, i=i: e.activation(GT[:, i, 24:28], banks[b][:, 280:284], ACT.Copy, scale=0.5), t0, *entry)
                gate_t[i] = [t1, t2]
                bank_free[b] = [ta, tb, t1, t2]
                b2 = bank()
                for k in range(4):
                    t = C.pe(lambda e, b2=b2, k=k, j=j: e.transpose(banks[b2][:, k * P:(k + 1) * P], stg[:, j, k * P:(k + 1) * P], ident),
                             ta, tb, *bank_free[b2], inc=(k == 3))
                stg_free[cnt[0]] = [t]
                src = banks[b2][:].rearrange("p (k c) -> p k c", k=4)
                tc = C.act(lambda e, i=i, src=src: e.activation(A[0:64, :, i * P:(i + 1) * P], src[0:64], ACT.Copy), t)
                if i == 0:
                    td = C.dve(lambda e, src=src: e.tensor_copy(A[64:128, :, 0:127], src[64:128, :, 1:128]), t, tc, *entry)
                else:
                    td = C.dve(lambda e, i=i, src=src: e.tensor_copy(A[64:128, :, i * P - 1:(i + 1) * P - 1], src[64:128]), t, tc)
                bank_free[b2] = [tc, td]
                at[i] = [tc, td]
                cnt[0] += 1
            release(u, t0)
            a_tok = [t for i in range(NT) for t in at[i]] + [tz]
            u = load(wnext()[:, 0:8 * 384], 8 * 384)
            w = u.ap.rearrange("p (k n) -> p k n", k=KT)
            vt = {}
            for i in range(NT):
                b = bank()
                t = mm_group(banks[b][:, 0:384], [(xT[:, k, i * P:(i + 1) * P], w[:, k, :]) for k in range(KT)], True,
                             u.tok, *bank_free[b], *res[i])
                vt[i] = C.act(lambda e, b=b, i=i: e.activation(V[:, i, :], banks[b][:, 0:384], ACT.Copy), t, *entry)
                bank_free[b] = [vt[i]]
            release(u, t)
            zfree = [C.last("pe"), C.last("dve"), C.last("act")]
            sm = Wk
            hid = ar(sm, 2 * 63).rearrange("p (m n) -> p m n", m=2)
            hraw = ar(sm + 832, 256)
            kcp = ar(sm + 128, 128)
            ksq = ar(sm + 256, 128)
            kro = ar(sm + 384, 256)
            cmpT = ar(sm + 640, 2 * 31).rearrange("p (g n) -> p g n", g=2)
            cmpV = ar(sm + 704, 128)
            out_ = {}
            DM, dm_t = {}, {}
            all_q = list(qkt.values())
            strip = cs("strip")
            m8 = mx8

            def side():
                cents = [C.last("dve"), C.last("act"), C.last("pe")]
                for kv in range(2):
                    u = cmp_u[kv]
                    w = u.ap.rearrange("p (j n) -> p j n", j=16)
                    pe_ = cs("kpe" if kv == 0 else "vpe")
                    b1 = cs("kb1" if kv == 0 else "vb1")
                    w2 = cs("kw2" if kv == 0 else "vw2").rearrange("p (k n) -> p k n", k=2)
                    b = bank()
                    for j in range(16):
                        C.pe(lambda e, b=b, j=j, kv=kv, w=w: e.matmul(
                            banks[b][0:63, 0:256], A.rearrange("p j s -> p (j s)")[:, 1024 * kv + 2 * j:1024 * kv + 2 * j + 993:16], w[:, j, :], start=(j == 0), stop=False),
                            u.tok, *a_tok, *bank_free[b], inc=False)
                    for j in range(16):
                        t = C.pe(lambda e, b=b, j=j, w=w, pe_=pe_: e.matmul(
                            banks[b][0:63, 0:256], pe_[:, j:j + 1].broadcast_to([P, 63]), w[:, j, :], start=False, stop=(j == 15)), inc=(j == 15))
                    release(u, t)
                    t = C.dve(lambda e, b=b: e.tensor_copy(hraw[0:63, :], banks[b][0:63, 0:256]), t, *cents)
                    bank_free[b] = [t]
                    yield
                    b = bank()
                    for m in range(2):
                        tp = C.pe(lambda e, b=b, m=m: e.transpose(banks[b][:, 63 * m:63 * m + 63], hraw[0:63, m * P:(m + 1) * P], ident[0:63, 0:63]),
                                  t, *bank_free[b], inc=(m == 1))
                    for m in range(2):
                        t = C.act(lambda e, b=b, m=m, b1=b1: e.activation(hid[:, m, :], banks[b][:, 63 * m:63 * m + 63], ACT.Silu, bias=b1[:, m:m + 1]), tp, *cents)
                    bank_free[b] = [t]
                    hb = [t]
                    yield
                    b = bank()
                    for g in range(2):
                        t = mm_group(banks[b][0:31, 64 * g:64 * g + 64], [(hid[:, m, g * 32:g * 32 + 31], w2[:, m, :]) for m in range(2)], True,
                                     *hb, *bank_free[b])
                    cents = [t]
                    dst = kcp if kv == 0 else cmpV
                    tv = C.dve(lambda e, b=b, dst=dst: e.tensor_copy(dst[0:31, :], banks[b][0:31, 0:128]), t, hb[-1])
                    bank_free[b] = [tv]
                    if kv == 0:
                        t = head_norm(kcp[0:31, :], ksq[0:31, :], hgc[0:31, :], 2, 31, ssq[0:31, 0:2], tv, t_hg)
                        kr2 = kro[0:31, :].rearrange("p (n r c) -> p n r c", n=2, r=2)
                        t = rope_block(kcp[0:31, :], ksq2[0:31, :], 2, cs("ccos")[0:31, :], cs("csin")[0:31, :], ksq[0:31, :], 31, t)
                        k3 = ksq2[0:31, :].rearrange("p (n c) -> p n c", c=64)
                        C.dve(lambda e, kr2=kr2, k3=k3: e.tensor_copy(kr2[:, :, 0, :], k3), t)
                        t = C.dve(lambda e, kr2=kr2, k3=k3: e.tensor_copy(kr2[:, :, 1, :], k3), t)
                        yield
                        b = bank()
                        for g in range(2):
                            tp = C.pe(lambda e, b=b, g=g: e.transpose(banks[b][:, 31 * g:31 * g + 31], kro[0:31, g * P:(g + 1) * P], ident[0:31, 0:31]),
                                      t, *bank_free[b], inc=(g == 1))
                        out_['T'] = C.dve(lambda e, b=b: e.tensor_copy(ar(sm + 640, 62), banks[b][:, 0:62]), tp)
                        bank_free[b] = [out_['T']]
                    else:
                        out_['V'] = tv

                o = DMo
                for i in range(1, NT):
                    DM[i] = ar(o, (i + 1) * P)
                    o += (i + 1) * P
                assert o <= Wk
                af = [C.last("pe"), C.last("dve"), C.last("act")]
                RL = [ar(15360 + 512 * j, 512) for j in range(2)]
                rl_free = {}
                n_rl = 0
                for i in range(1, NT):
                    nk = (i + 1) * P
                    t = None
                    for hd in range(4):
                        b = bank()
                        base = 64 * (hd % 2)
                        tm = C.pe(lambda e, b=b, base=base, hd=hd, i=i, nk=nk: e.matmul(
                            banks[b][:, 0:nk], QK[base:base + 64, 14 + hd // 2, i * P:(i + 1) * P], QK[base:base + 64, 16, 0:nk], start=True, stop=True),
                            *all_q, *bank_free[b])
                        j = n_rl % 2
                        tr = C.act(lambda e, b=b, j=j, nk=nk: e.activation(RL[j][:, 0:nk], banks[b][:, 0:nk], ACT.Relu, scale=0.125), tm, *rl_free.get(n_rl - 2, []), *af)
                        bank_free[b] = [tr]
                        wi_ = GT[:, i, 24 + hd:25 + hd]
                        if hd == 0:
                            t = C.dve(lambda e, j=j, nk=nk, wi_=wi_, i=i: e.tensor_scalar(DM[i], RL[j][:, 0:nk], wi_, None, ALU.mult), tr, *gate_t[i], *af)
                        else:
                            t = C.dve(lambda e, j=j, nk=nk, wi_=wi_, i=i: e.scalar_tensor_tensor(DM[i], RL[j][:, 0:nk], wi_, DM[i], ALU.mult, ALU.add), tr, t)
                        rl_free[n_rl] = [t]
                        n_rl += 1
                        yield
                    so_ = strip[:, 384 - P * i:512]
                    t = C.dve(lambda e, i=i, so_=so_: e.tensor_tensor(DM[i], DM[i], so_, ALU.add), t)
                    dm_t[i] = t


            def dm_steps():
                for i in range(1, NT):
                    t = dm_t[i]
                    for _ in range(16):
                        t = C.dve(lambda e, i=i: e.max(m8[:, i, :], DM[i]), t)
                        t = C.dve(lambda e, i=i: e.match_replace(DM[i], m8[:, i, :], DM[i], -3e30), t)
                        yield
                    so_ = strip[:, 384 - P * i:512]
                    t = C.dve(lambda e, i=i: e.tensor_scalar(DM[i], DM[i], -2.5e30, NEG, ALU.is_gt, ALU.mult), t)
                    dm_t[i] = C.dve(lambda e, i=i, so_=so_: e.tensor_tensor(DM[i], DM[i], so_, ALU.min), t)
                    yield


            steps = dm_steps()
            sides = side()
            at_side = [True]

            def aside(n):
                for _ in range(n):
                    if at_side[0] and next(sides, StopIteration) is StopIteration:
                        at_side[0] = False
                    if not at_side[0]:
                        next(steps, None)
                        next(steps, None)

            cmp_u = [load(wnext()), load(wnext())]
            aside(2)
            zt = {}
            for c in range(2):
                u = load(wnext())
                w = u.ap.rearrange("p (k n) -> p k n", k=KT)
                for i in range(NT):
                    b = bank()
                    t = mm_group(banks[b][:], [(xT[:, k, i * P:(i + 1) * P], w[:, k, :]) for k in range(KT)], True,
                                 u.tok, *bank_free[b], *res[i])
                    zt[(c, i)] = C.act(lambda e, b=b, i=i, c=c: e.activation(Z[:, i, 512 * c:512 * c + 512], banks[b][:], ACT.Silu), t, *zfree)
                    bank_free[b] = [zt[(c, i)]]
                    aside(3)
                release(u, t)
            proj_done = C.last("pe")

            while at_side[0]:
                aside(1)
            t_cmpT, t_cmpV = out_["T"], out_["V"]
            scratch = reserve()
            DEEP = 4
            sc = [scratch.ap[:, 512 * j:512 * j + 512] for j in range(DEEP)]
            PTb = [scratch.ap[:, 512 * (DEEP + j):512 * (DEEP + j + 1)] for j in range(DEEP)]
            w_out = [load(wnext()), load(wnext())]
            MX = ar(0, 4096).rearrange("p (t c) -> p t c", t=NT)
            st = small[:, 24:56]
            state = dict(n=0)
            free_s, free_pt, mx_t, free_c = {}, {}, {}, {}

            def branch(i, qh, qpair, kp, v_ap, mask, col, coef, nkeys, mul=None, first=True, vtoks=(), cmp=False):
                n = state["n"]
                state["n"] += 1
                j = n % DEEP
                base = 64 * (qh % 2)
                b, b2, b3 = n % 3, 3 + n % 3, 6 + n % 2
                krhs = cmpT[base:base + 64, kp, :] if cmp else QK[base:base + 64, kp, 0:nkeys]
                tm = C.pe(lambda e: e.matmul(banks[b][:, 0:nkeys], QK[base:base + 64, qpair, i * P:(i + 1) * P], krhs, start=True, stop=True),
                          *all_q, *bank_free[b], *([t_cmpT] if cmp else []))
                s_ = sc[j][:, 0:nkeys]
                nm = st[:, n % 8:n % 8 + 1]
                lrow = st[:, 8 + n % 8:9 + n % 8]
                cf = st[:, 16 + n % 8:17 + n % 8]
                nb = (nkeys + P - 1) // P
                yield
                mk, mtok = mask()
                t = C.dve(lambda e: e.tensor_tensor_reduce(s_, banks[b][:, 0:nkeys], mk, -SCALE, 3e38, ALU.add, ALU.min, nm),
                          tm, *mtok, *free_s.get(n - DEEP, []), *scratch.free)
                bank_free[b] = [t]
                te = C.act(lambda e: e.activation(s_, s_, ACT.Exp, bias=nm, scale=-1.0, accum_out=lrow), t)
                yield
                yield
                t = te
                if mul is not None:
                    t = C.dve(lambda e: e.tensor_tensor(s_, s_, mul, ALU.mult), te)
                for k in range(nb):
                    w_ = min(P, nkeys - k * P)
                    tp = C.pe(lambda e, k=k, w_=w_: e.transpose(banks[b2][0:w_, k * P:(k + 1) * P], s_[:, k * P:k * P + w_], ident),
                              t, *bank_free[b2], inc=(k == nb - 1))
                free_s[n] = [tp]
                t2 = C.dve(lambda e: e.reciprocal(cf, lrow), te)
                if coef is not None:
                    t2 = C.dve(lambda e: e.tensor_tensor(cf, cf, coef, ALU.mult), t2, *gate_t[i])
                yield
                rows = min(P, nkeys)
                te2 = C.act(lambda e: e.activation(PTb[j][0:rows, 0:nb * P], banks[b2][0:rows, 0:nb * P], ACT.Copy), tp, *free_pt.get(n - DEEP, []), *scratch.free)
                bank_free[b2] = [te2]
                yield
                for k in range(nb):
                    w_ = min(P, nkeys - k * P)
                    tq = C.pe(lambda e, k=k, w_=w_: e.matmul(banks[b3][:, 0:64], PTb[j][0:w_, k * P:(k + 1) * P], v_ap(k), start=(k == 0), stop=(k == nb - 1)),
                              te2, *vtoks, *bank_free[b3], inc=(k == nb - 1))
                free_pt[n] = [tq]
                yield
                dst = MX[:, i, col:col + 64]
                if first:
                    to = C.dve(lambda e: e.tensor_scalar(dst, banks[b3][:, 0:64], cf, None, ALU.mult), tq, t2, proj_done)
                else:
                    to = C.dve(lambda e: e.scalar_tensor_tensor(dst, banks[b3][:, 0:64], cf, dst, ALU.mult, ALU.add), tq, t2, mx_t[(i, col)])
                bank_free[b3] = [to]
                mx_t[(i, col)] = to
                free_c[n] = [to]

            vts = [vt[i] for i in range(NT)]
            cadd = cs("cmpadd").rearrange("p (t n) -> p t n", t=NT)
            cmul = cs("cmpmul").rearrange("p (t n) -> p t n", t=NT)
            work = []
            for i in range(NT):
                nk = (i + 1) * P
                caus = (strip[:, 384 - P * i:512], [])
                for hd in range(8):
                    g = hd // 4
                    gc = lambda r, hd=hd, i=i: GT[:, i, 3 * hd + r:3 * hd + r + 1]
                    work.append(lambda i=i, hd=hd, g=g, gc=gc: branch(i, hd, hd // 2, g, lambda k, g=g: cmpV[0:31, 64 * g:64 * g + 64],
                                lambda i=i: (cadd[:, i, :], []), 64 * hd, gc(0), 31, mul=cmul[:, i, :], first=True, vtoks=[t_cmpV], cmp=True))
                    work.append(lambda i=i, hd=hd, g=g, gc=gc, nk=nk, caus=caus: branch(i, hd, hd // 2, 8 + g, lambda k, g=g: V[:, k, 64 * g:64 * g + 64],
                                lambda caus=caus: caus, 64 * hd, gc(1), nk, first=False, vtoks=vts))
                    work.append(lambda i=i, hd=hd, g=g, gc=gc, nk=nk, caus=caus: branch(i, hd, hd // 2, 10 + g, lambda k, g=g: V[:, k, 128 + 64 * g:192 + 64 * g],
                                lambda caus=caus: caus, 64 * hd, gc(2), nk, first=False, vtoks=vts))
            n_nsa = len(work)
            for i in range(NT):
                nk = (i + 1) * P
                caus = (strip[:, 384 - P * i:512], [])
                for hd in range(8):
                    g = hd // 4
                    mk = lambda i=i, caus=caus: caus if i == 0 else (DM[i], [dm_t[i]])
                    work.append(lambda i=i, hd=hd, g=g, nk=nk, mk=mk: branch(i, hd, 4 + hd // 2, 12 + g, lambda k, g=g: V[:, k, 256 + 64 * g:320 + 64 * g],
                                mk, 512 + 64 * hd, None, nk, first=True, vtoks=vts))
            live = []
            for n_ in range(len(work) + 8):
                if n_ == n_nsa:
                    for _ in steps:
                        pass
                live = [x for x in live if next(x, StopIteration) is not StopIteration]
                if n_ < len(work):
                    x = work[n_]()
                    next(x)
                    live.append(x)
                if n_ % 2:
                    next(steps, None)
            assert not live

            mT = ar(4096, 4096).rearrange("p (k s) -> p k s", k=KT)
            done_qk = [C.last("pe"), C.last("act")]
            mt = []
            for i in range(NT):
                t = C.dve(lambda e, i=i: e.tensor_tensor(MX[:, i, :], MX[:, i, :], Z[:, i, :], ALU.mult), C.last("dve"), zt[(0, i)], zt[(1, i)])
                C.wait("dve", *done_qk)
                d_, _ = transposed(mT, MX[:, i, :], [t], i)
                mt += d_
            us = w_out
            l_o = Lane(nc, ctx, "l_o")
            for i in range(NT):
                for c in range(2):
                    u = us[c]
                    w = u.ap.rearrange("p (k n) -> p k n", k=KT)
                    b = bank()
                    t = mm_group(banks[b][:], [(mT[:, k, i * P:(i + 1) * P], w[:, k, :]) for k in range(KT)], True,
                                 u.tok, *bank_free[b], *mt)
                    t = add_to_h(i, 512 * c, 512, b, t)
                to = l_o.dma(C, "pool", lambda e, i=i: e.dma_start(t_["out"][i * P:(i + 1) * P, :], h[:, i, :]), t)
            for e in C.q:
                C.wait(e, to)

        def store_rows(l, xs_t):
            lanes = [Lane(nc, ctx, f"l_xs{l}_{i}") for i in range(NT)]

            def go(i, src, t):
                xs_t.append(lanes[i].dma(C, "pool", lambda e: e.dma_start(xs_d[l][i * P:(i + 1) * P, :], src), t))
                return [xs_t[-1]]
            return go

        xs_t = [[], []]
        n0 = Norm(0, ar(8192, 2048), ar(10240, 1024), toks=arena_free)
        n1 = Norm(1, ar(16384, 4096), ar(10240, 1024), also=store_rows(0, xs_t[0]))
        mixer_a(n0, n1)
        n2 = Norm(2, ar(4096, 2048), ar(6144, 1024))
        moe(0, n1, n2, xs_t[0])
        n3 = Norm(3, ar(20480, 2048), ar(22528, 1024), toks=cy_t)
        ple(0, n2, n3)
        n4 = Norm(4, ar(16384, 4096), ar(10240, 1024), also=store_rows(1, xs_t[1]))
        mixer_b(n3, n4)
        n5 = Norm(5, ar(4096, 2048), ar(6144, 1024))
        moe(1, n4, n5, xs_t[1])
        n7 = Norm(7, ar(20480, 2048), ar(22528, 1024), first=Norm(6, None, ar(22528, 1024)))
        ple(1, n5, n7)
        attention(n7)
        assert wat[0] == W.shape[0], (wat[0], W.shape)

        block = ctx.enter_context(nc.Block())
        for deco, name in ((block.sync, "sp"), (block.tensor, "pe"), (block.vector, "dve"), (block.scalar, "act"), (block.gpsimd, "pool")):
            @deco
            def _(e, name=name):
                for f in C.q[name]:
                    f(e)


def _units(w, widths=None):
    K, N = w.shape
    out, a = [], 0
    for n in (widths or [512] * (N // 512)):
        u = w[:, a:a + n].reshape(K // P, P, n).transpose(1, 0, 2).reshape(P, -1)
        if u.shape[1] < UNIT:
            u = np.concatenate([u, np.zeros((P, UNIT - u.shape[1]), u.dtype)], axis=1)
        out.append(u)
        a += n
    return out


def _cols(v, n):
    return np.moveaxis(v.reshape(*v.shape[:-1], n, P), -1, 0).reshape(P, -1)


def _shape_tables():
    f = np.float32
    tb = {}
    tb["ident"] = np.eye(P, dtype=f)
    tb["tri"] = np.triu(np.ones((P, P), f), 1)
    p = np.arange(P)[:, None]
    tb["strip"] = np.where(np.arange(512)[None, :] <= p + 384, 0.0, NEG).astype(f)
    tb["ones"] = np.ones((P, 128), f)
    t = np.arange(S).reshape(NT, P).T[:, :, None]
    end = (np.arange(NCMP) * 16 + 31)[None, None, :]
    tb["cmpmul"] = (end <= t).astype(f).reshape(P, -1)
    tb["cmpadd"] = np.where(end <= t, 0.0, NEG).astype(f).reshape(P, -1)
    inv = (f(10000.0) ** (-np.arange(32, dtype=f) / f(32))).astype(f)
    ang = (t.astype(f) * inv[None, None, :]).astype(f)
    tb["cos"], tb["sin"] = np.cos(ang).reshape(P, -1), np.sin(ang).reshape(P, -1)
    ca = np.zeros((P, 32), f)
    ca[:NCMP] = (np.arange(NCMP) * 16 + 31).astype(f)[:, None] * inv[None, :]
    tb["ccos"], tb["csin"] = np.cos(ca), np.sin(ca)
    tb["rev4"] = np.tile(np.arange(4, 0, -1).astype(f), (P, 1))
    tb["rev8"] = np.tile(np.arange(8, 0, -1).astype(f), (P, 1))
    tb["iota32"] = np.tile(np.arange(NE).astype(f), (P, 1))
    tb["iotab"] = np.tile(np.arange(NOVF).astype(f), (P, 1))
    tb["iotas"] = np.tile(np.arange(CAP).astype(f), (P, 1))
    tb["tok"] = np.arange(S).reshape(NT, P).T.astype(f)
    return tb


def kernel(**inputs):
    import concourse.bacc as _bacc
    from concourse.bass_utils import run_bass_kernel_spmd as _run

    v = {k: np.asarray(a) for k, a in inputs.items()}
    tb = _shape_tables()
    tb["conva"] = _cols(v["conv_a"][0], 8).reshape(P, 3, 8).transpose(0, 2, 1).reshape(P, -1)
    tb["convb"] = _cols(v["conv_b"][0], 8).reshape(P, 4, 8).transpose(0, 2, 1).reshape(P, -1)
    tb["cbias"] = _cols(v["conv_bias_b"][0], 8)
    tb["br"], tb["bi"], tb["lam"] = (_cols(v[k][0], 8) for k in ("b_rgate_b", "b_igate_b", "lam_b"))
    for kv in "kv":
        tb[f"{kv}b1"] = _cols(v[f"cmp_{kv}_b1_2"][0], 2)
        tb[f"{kv}pe"] = v[f"cmp_pe_{kv}_2"][0].reshape(16, P).T
        tb[f"{kv}w2"] = v[f"cmp_{kv}_w2_2"][0].reshape(2, P, 64).transpose(1, 0, 2).reshape(P, -1)
    rb = []
    for l in range(2):
        rw = np.concatenate([v["w_router_group"][l], v["w_router_expert"][l]], axis=1)
        tb[f"rw{l}"] = rw.reshape(KT, P, 36).transpose(1, 0, 2).reshape(P, -1)
        rb += [v["b_router_group"][l], v["b_router_expert"][l]]
    tb["rb"] = np.broadcast_to(np.concatenate(rb), (P, 72))
    cst = np.concatenate([tb[n].reshape(P, w) for n, w in CST], axis=1)
    rows = np.stack([v["norm_mix"][0], v["norm_ffn"][0], v["norm_ple"][0], v["norm_mix"][1], v["norm_ffn"][1],
                     v["norm_ple"][1], v["norm_final"], v["norm_gain_2"][0]])
    q, ks, kw, kc, qd, kd = (v[k][0] for k in ("nsa_q_gain_2", "nsa_ks_gain_2", "nsa_kw_gain_2", "nsa_kc_gain_2", "dsa_q_gain_2", "dsa_k_gain_2"))
    hgain = np.concatenate([q] * 8 + [qd] * 8 + [ks] * 2 + [kw] * 2 + [kd] * 2 + [kc] * 2)[None, :]

    wall = []
    wa = _units(v["w_in_a"][0])
    for c in range(2):
        wall += [wa[c], wa[2 + c], wa[4 + c]]
    wall += _units(v["w_out_a"][0])

    def ple_units(l):
        return _units(v["w_ple"][l], [1024]) + _units(v["w_ple_gate"][l])

    wall += ple_units(0)
    wb = _units(v["w_in_b"][0])
    gates = np.stack([v["w_rgate_b"][0], v["w_igate_b"][0]], axis=1)
    wall += wb[2:]
    for d in range(2):
        wall.append(gates[d].reshape(2, 4, 2, P, 256).transpose(3, 0, 1, 2, 4).reshape(P, -1))
        wall.append(wb[d])
    wall += _units(v["w_out_b"][0])
    wall += ple_units(1)
    w2 = v["w_in_2"][0]
    at, a = {}, 0
    for name, n in (("q_n", 512), ("kc", 128), ("vc", 128), ("ks", 128), ("vs", 128), ("kw", 128), ("vw", 128), ("gate", 24),
                    ("z_n", 512), ("q_d", 512), ("k_d", 128), ("v_d", 128), ("qi", 256), ("ki", 64), ("wi", 4), ("z_d", 512)):
        at[name] = w2[:, a:a + n]
        a += n
    for names in (["q_n"], ["q_d"], ["ks", "kw", "k_d"], ["qi", "ki"], ["kc", "vc", "gate", "wi"], ["vs", "vw", "v_d"], "kv", ["z_n"], ["z_d"]):
        if names == "kv":
            for kv in "kv":
                wall.append(v[f"cmp_{kv}_w1_2"][0].reshape(16, P, 256).transpose(1, 0, 2).reshape(P, -1))
            continue
        m = np.concatenate([at[x] for x in names], axis=1)
        wall += _units(m, [m.shape[1]])
    wall += _units(v["w_out_2"][0])
    wall = np.stack(wall)

    wexp = np.empty((2, NE, 3, P, UNIT), np.float32)
    wexp[:, :, 0] = v["w_exp_gate"].reshape(2, NE, KT, P, 512).transpose(0, 1, 3, 2, 4).reshape(2, NE, P, UNIT)
    wexp[:, :, 1] = v["w_exp_up"].reshape(2, NE, KT, P, 512).transpose(0, 1, 3, 2, 4).reshape(2, NE, P, UNIT)
    wexp[:, :, 2] = v["w_exp_down"].reshape(2, NE, 4, P, D).transpose(0, 1, 3, 2, 4).reshape(2, NE, P, UNIT)

    arrays = {
        "x": v["x"][0], "cst": cst, "rows": rows, "hgain": hgain, "wall": wall, "wexp": wexp,
        "pT": v["p"][:, 0].transpose(0, 2, 1).reshape(2, 2, P, S).transpose(0, 2, 1, 3).reshape(2, P, 2 * S),
        "plebias": v["b_ple_gate"],
    }
    arrays = {k: np.ascontiguousarray(a) for k, a in arrays.items()}
    nc = _bacc.Bacc("TRN2", target_bir_lowering=False, num_devices=1)
    t_ = {k: nc.dram_tensor(f"in_{k}", a.shape, mybir.dt.from_np(a.dtype), kind="ExternalInput").ap() for k, a in arrays.items()}
    t_["out"] = nc.dram_tensor("out_0", (S, D), F32, kind="ExternalOutput").ap()
    build(nc, t_)
    r = _run(nc, [{f"in_{k}": a for k, a in arrays.items()}], core_ids=[0])
    return r.results[0]["out_0"].reshape(1, S, D)
```
